# Optimizing a Trainium2 kernel written in Bass

```python
import math
import jax
import jax.numpy as jnp
from jax import lax
import numpy as np
import jax, jax.numpy as jnp

D_MODEL = 1024
BATCH = 1
SEQ = 256
DEPTH = 2

HEAD_DIM = 64
DIFF_W = (D_MODEL * 3 // 8)
DELTA_W = (D_MODEL * 3 // 8)
CONV_CH = D_MODEL - DIFF_W - DELTA_W
DIFF_HEADS = DIFF_W // HEAD_DIM
DIFF_DIM = HEAD_DIM // 2
DELTA_HEADS = DELTA_W // HEAD_DIM
CONV_WIDTH = 31
SHORT_CONV = 3
CHUNK = 64
Q_BLOCK = 128
D_FF = 4 * D_MODEL
IN_W = 2 * CONV_CH + 3 * DIFF_W + 4 * DELTA_W + 4 * DELTA_HEADS
NORM_EPS = 1e-6


def rms_norm(x, w, eps=NORM_EPS):
    xf = x.astype(jnp.float32)
    y = xf * lax.rsqrt(jnp.mean(xf * xf, axis=-1, keepdims=True) + eps)
    return (y * w.astype(jnp.float32)).astype(x.dtype)

def layer_norm(x, w, b, eps=1e-5):
    xf = x.astype(jnp.float32)
    mu = jnp.mean(xf, axis=-1, keepdims=True)
    xc = xf - mu
    var = jnp.mean(xc * xc, axis=-1, keepdims=True)
    y = xc * lax.rsqrt(var + eps) * w.astype(jnp.float32) + b.astype(jnp.float32)
    return y.astype(x.dtype)

def l2norm(x, eps=1e-6):
    xf = x.astype(jnp.float32)
    return xf * lax.rsqrt(jnp.sum(xf * xf, axis=-1, keepdims=True) + eps)

def depthwise_conv(x, w):
    k, c = w.shape
    pad = (k - 1) // 2
    return lax.conv_general_dilated(
        x, w[:, None, :].astype(x.dtype), window_strides=(1,), padding=[(pad, pad)],
        dimension_numbers=("NWC", "WIO", "NWC"), feature_group_count=c)

def alibi_slopes(n):
    def pow2(m):
        start = 2.0 ** (-8.0 / m)
        return [start ** (i + 1) for i in range(m)]
    if math.log2(n).is_integer():
        s = pow2(n)
    else:
        c = 2 ** int(math.floor(math.log2(n)))
        s = pow2(c) + pow2(2 * c)[0::2][: n - c]
    return jnp.asarray(s, dtype=jnp.float32)

def conv_module(u, dw_w, dw_b, ln_w, ln_b):
    a, g = jnp.split(u, 2, axis=-1)
    h = a * jax.nn.sigmoid(g)
    h = depthwise_conv(h, dw_w) + dw_b.astype(h.dtype)
    h = layer_norm(h, ln_w, ln_b)
    return jax.nn.silu(h)

def diff_attention(q, k, v, lam_q1, lam_k1, lam_q2, lam_k2, subln_w, layer_idx):
    B, S = q.shape[0], q.shape[1]
    H = DIFF_HEADS
    f32 = jnp.float32
    lambda_init = 0.8 - 0.6 * math.exp(-0.3 * layer_idx)
    lam = (jnp.exp(jnp.sum(lam_q1.astype(f32) * lam_k1.astype(f32)))
           - jnp.exp(jnp.sum(lam_q2.astype(f32) * lam_k2.astype(f32))) + lambda_init)
    slopes = jnp.repeat(alibi_slopes(H), 2)
    n_blk = S // Q_BLOCK
    qf = q.astype(f32).reshape(B, n_blk, Q_BLOCK, 2 * H, DIFF_DIM) * (DIFF_DIM ** -0.5)
    qf = jnp.moveaxis(qf, 1, 0)
    kf = k.astype(f32).reshape(B, S, 2 * H, DIFF_DIM)
    vf = v.astype(f32).reshape(B, S, H, HEAD_DIM)
    kpos = jnp.arange(S)

    def block(args):
        q_blk, blk = args
        s = jnp.einsum("bqmd,bkmd->bmqk", q_blk, kf)
        qpos = blk * Q_BLOCK + jnp.arange(Q_BLOCK)
        dist = jnp.abs(qpos[:, None] - kpos[None, :]).astype(f32)
        p = jax.nn.softmax(s - slopes[:, None, None] * dist, axis=-1)
        p = p.reshape(B, H, 2, Q_BLOCK, S)
        a = p[:, :, 0] - lam * p[:, :, 1]
        return jnp.einsum("bhqk,bkhe->bqhe", a, vf)

    o = lax.map(block, (qf, jnp.arange(n_blk)))
    o = jnp.moveaxis(o, 0, 1).reshape(B, S, H, HEAD_DIM)
    o = rms_norm(o, subln_w, eps=1e-5) * (1.0 - lambda_init)
    return o.reshape(B, S, H * HEAD_DIM).astype(q.dtype)

def chunk_gated_delta(q, k, v, g, beta):
    B, S, H, Dk = q.shape
    Dv = v.shape[-1]
    N = S // CHUNK
    q = q * (Dk ** -0.5)

    def chunks(t):
        return t.reshape(B, N, CHUNK, H, -1).transpose(0, 3, 1, 2, 4)

    qc, kc, vc = chunks(q), chunks(k), chunks(v)
    gc = jnp.cumsum(g.reshape(B, N, CHUNK, H).transpose(0, 3, 1, 2), axis=-1)
    bc = beta.reshape(B, N, CHUNK, H).transpose(0, 3, 1, 2)
    idx = jnp.arange(CHUNK)
    lower = idx[:, None] >= idx[None, :]
    strict = idx[:, None] > idx[None, :]
    decay = jnp.exp(jnp.where(lower, gc[..., :, None] - gc[..., None, :], -jnp.inf))
    kb = kc * bc[..., None]
    A = jnp.where(strict, jnp.einsum("bhncd,bhnsd->bhncs", kb, kc) * decay, 0.0)
    rhs = jnp.concatenate([vc * bc[..., None], kb * jnp.exp(gc)[..., None]], axis=-1)
    sol = lax.linalg.triangular_solve(A, rhs, left_side=True, lower=True, unit_diagonal=True)
    u, w = sol[..., :Dv], sol[..., Dv:]
    Aqk = jnp.einsum("bhncd,bhnsd->bhncs", qc, kc) * decay
    qg = qc * jnp.exp(gc)[..., None]
    kdec = kc * jnp.exp(gc[..., -1:] - gc)[..., None]
    glast = jnp.exp(gc[..., -1])

    def step(state, inp):
        u_i, w_i, qg_i, aqk_i, kdec_i, gl_i = inp
        v_new = u_i - jnp.einsum("bhcd,bhde->bhce", w_i, state)
        o = jnp.einsum("bhcd,bhde->bhce", qg_i, state) + jnp.einsum("bhcs,bhse->bhce", aqk_i, v_new)
        state = state * gl_i[..., None, None] + jnp.einsum("bhcd,bhce->bhde", kdec_i, v_new)
        return state, o

    xs = tuple(jnp.moveaxis(t, 2, 0) for t in (u, w, qg, Aqk, kdec, glast))
    s0 = jnp.zeros((B, H, Dk, Dv), jnp.float32)
    _, o = lax.scan(step, s0, xs)
    return o.transpose(1, 0, 3, 2, 4).reshape(B, S, H, Dv)

def gated_deltanet(qkv, z, b_f, b_b, a_f, a_b, conv_w, A_log, dt_bias, norm_w):
    B, S, _ = qkv.shape
    H, D = DELTA_HEADS, HEAD_DIM
    f32 = jnp.float32
    out_dtype = qkv.dtype
    qkv = jax.nn.silu(depthwise_conv(qkv, conv_w))
    q, k, v = jnp.split(qkv, 3, axis=-1)
    q = l2norm(q.reshape(B, S, H, D))
    k = l2norm(k.reshape(B, S, H, D))
    v = v.reshape(B, S, H, D).astype(f32)

    def log_decay(a, a_log, dtb):
        return -jnp.exp(a_log.astype(f32)) * jax.nn.softplus(a.astype(f32) + dtb.astype(f32))

    g_f = log_decay(a_f, A_log[0], dt_bias[0])
    g_b = log_decay(a_b, A_log[1], dt_bias[1])
    beta_f = jax.nn.sigmoid(b_f.astype(f32))
    beta_b = jax.nn.sigmoid(b_b.astype(f32))
    o_f = chunk_gated_delta(q, k, v, g_f, beta_f)
    rev = lambda t: jnp.flip(t, axis=1)
    o_b = rev(chunk_gated_delta(rev(q), rev(k), rev(v), rev(g_b), rev(beta_b)))
    o = rms_norm(o_f + o_b, norm_w) * jax.nn.silu(z.astype(f32).reshape(B, S, H, D))
    return o.reshape(B, S, H * D).astype(out_dtype)

def first_inputs(seed: int = 0) -> dict:
    key = jax.random.key(seed)
    ks = jax.random.split(key, 24)
    f32 = jnp.float32
    nrm = lambda k, shape, scale: jax.random.normal(k, shape, f32) * scale
    gain = lambda k, shape: 1.0 + 0.05 * jax.random.normal(k, shape, f32)
    dt = jnp.exp(jax.random.uniform(ks[20], (DEPTH, 2, DELTA_HEADS), f32, math.log(1e-3), math.log(1e-1)))
    return {
        "x": nrm(ks[0], (BATCH, SEQ, D_MODEL), 1.0),
        "w_in": nrm(ks[1], (DEPTH, D_MODEL, IN_W), D_MODEL ** -0.5),
        "w_out": nrm(ks[2], (DEPTH, D_MODEL, D_MODEL), D_MODEL ** -0.5),
        "pre_mix_w": gain(ks[3], (DEPTH, D_MODEL)),
        "post_mix_w": gain(ks[4], (DEPTH, D_MODEL)),
        "pre_mlp_w": gain(ks[5], (DEPTH, D_MODEL)),
        "post_mlp_w": gain(ks[6], (DEPTH, D_MODEL)),
        "w_ff1": nrm(ks[7], (DEPTH, D_MODEL, D_FF), D_MODEL ** -0.5),
        "w_ff2": nrm(ks[8], (DEPTH, D_FF, D_MODEL), D_FF ** -0.5),
        "conv_dw_w": nrm(ks[9], (DEPTH, CONV_WIDTH, CONV_CH), CONV_WIDTH ** -0.5),
        "conv_dw_b": nrm(ks[10], (DEPTH, CONV_CH), 0.02),
        "conv_ln_w": gain(ks[11], (DEPTH, CONV_CH)),
        "conv_ln_b": nrm(ks[12], (DEPTH, CONV_CH), 0.02),
        "diff_lambda_q1": nrm(ks[13], (DEPTH, DIFF_DIM), 0.1),
        "diff_lambda_k1": nrm(ks[14], (DEPTH, DIFF_DIM), 0.1),
        "diff_lambda_q2": nrm(ks[15], (DEPTH, DIFF_DIM), 0.1),
        "diff_lambda_k2": nrm(ks[16], (DEPTH, DIFF_DIM), 0.1),
        "diff_subln_w": gain(ks[17], (DEPTH, HEAD_DIM)),
        "delta_conv_w": nrm(ks[18], (DEPTH, SHORT_CONV, 3 * DELTA_W), SHORT_CONV ** -0.5),
        "delta_A_log": jnp.log(jax.random.uniform(ks[19], (DEPTH, 2, DELTA_HEADS), f32, 1.0, 16.0)),
        "delta_dt_bias": dt + jnp.log(-jnp.expm1(-dt)),
        "delta_norm_w": gain(ks[21], (DEPTH, HEAD_DIM)),
    }

def first_block(x, w_in, w_out, pre_mix_w, post_mix_w, pre_mlp_w, post_mlp_w, w_ff1, w_ff2,
              conv_dw_w, conv_dw_b, conv_ln_w, conv_ln_b,
              diff_lambda_q1, diff_lambda_k1, diff_lambda_q2, diff_lambda_k2, diff_subln_w,
              delta_conv_w, delta_A_log, delta_dt_bias, delta_norm_w):
    sizes = [2 * CONV_CH, DIFF_W, DIFF_W, DIFF_W, 3 * DELTA_W, DELTA_W,
             DELTA_HEADS, DELTA_HEADS, DELTA_HEADS, DELTA_HEADS]
    offs = [sum(sizes[: i + 1]) for i in range(len(sizes) - 1)]
    for l in range(DEPTH):
        h = rms_norm(x, pre_mix_w[l])
        u = h @ w_in[l]
        (u_conv, dq, dk, dv, gqkv, gz, b_f, b_b, a_f, a_b) = jnp.split(u, offs, axis=-1)
        y_conv = conv_module(u_conv, conv_dw_w[l], conv_dw_b[l], conv_ln_w[l], conv_ln_b[l])
        y_diff = diff_attention(dq, dk, dv, diff_lambda_q1[l], diff_lambda_k1[l],
                                diff_lambda_q2[l], diff_lambda_k2[l], diff_subln_w[l], l)
        y_delta = gated_deltanet(gqkv, gz, b_f, b_b, a_f, a_b, delta_conv_w[l],
                                 delta_A_log[l], delta_dt_bias[l], delta_norm_w[l])
        y = jnp.concatenate([y_conv, y_diff, y_delta], axis=-1) @ w_out[l]
        x = x + rms_norm(y, post_mix_w[l])
        h = rms_norm(x, pre_mlp_w[l])
        y = jnp.square(jax.nn.relu(h @ w_ff1[l])) @ w_ff2[l]
        x = x + rms_norm(y, post_mlp_w[l])
    return x


GRID_W = 64
CTX_LEN = 256
N_MIXERS = 2
N_MLA_LAYERS = (DEPTH + N_MIXERS - 1) // N_MIXERS
N_POOL_LAYERS = DEPTH // N_MIXERS
MLA_HEADS = 8
QK_NOPE_DIM = 128
QK_ROPE_DIM = 64
V_HEAD_DIM = 128
Q_LORA_RANK = 384
KV_LORA_RANK = 256
MLA_IN_DIM = Q_LORA_RANK + KV_LORA_RANK + QK_ROPE_DIM
ROPE_THETA = 10000.0
POOL_WINDOWS = (2, 4, 8, 16)
N_POOL_GROUPS = 4
POOL_GROUP_DIM = D_MODEL // N_POOL_GROUPS
PEER_HEADS = 8
PEER_N_KEYS = 128
PEER_N_EXPERTS = PEER_N_KEYS * PEER_N_KEYS
PEER_QUERY_DIM = 256
PEER_HALF = PEER_QUERY_DIM // 2
PEER_TOPK = 16
PEER_BLOCK = 128
LN_EPS = 1e-5
RMS_EPS = 1e-6
DEEPNORM_ALPHA = (2.0 * DEPTH) ** 0.25
DEEPNORM_BETA = (8.0 * DEPTH) ** -0.25
N_MOD = 6


def _layernorm(x, g, b):
    xf = x.astype(jnp.float32)
    mu = jnp.mean(xf, axis=-1, keepdims=True)
    var = jnp.mean(jnp.square(xf - mu), axis=-1, keepdims=True)
    return ((xf - mu) * lax.rsqrt(var + LN_EPS) * g + b).astype(x.dtype)

def _rmsnorm(x, g):
    xf = x.astype(jnp.float32)
    return (xf * lax.rsqrt(jnp.mean(jnp.square(xf), axis=-1, keepdims=True) + RMS_EPS) * g).astype(x.dtype)

def _axial_rope_tables(n_tokens):
    rows_n = n_tokens // GRID_W
    row = jnp.repeat(jnp.arange(rows_n), GRID_W).astype(jnp.float32)
    col = jnp.tile(jnp.arange(GRID_W), rows_n).astype(jnp.float32)
    n_freq = QK_ROPE_DIM // 4
    freqs = ROPE_THETA ** (-jnp.arange(n_freq, dtype=jnp.float32) / n_freq)
    ang = jnp.concatenate([row[:, None] * freqs, col[:, None] * freqs], axis=-1)
    return jnp.cos(ang), jnp.sin(ang)

def _apply_rope(x, cos, sin):
    half = x.shape[-1] // 2
    xf = x.astype(jnp.float32)
    x1, x2 = xf[..., :half], xf[..., half:]
    return jnp.concatenate([x1 * cos - x2 * sin, x1 * sin + x2 * cos], axis=-1).astype(x.dtype)

def _block_attention(q, k, v):
    b, s, h, dk = q.shape
    scale = dk ** -0.5
    qb = q.reshape(b, s // Q_BLOCK, Q_BLOCK, h, dk).transpose(1, 0, 2, 3, 4)

    def one(qblk):
        sc = jnp.einsum('bqhd,bkhd->bhqk', qblk, k, preferred_element_type=jnp.float32) * scale
        p = jax.nn.softmax(sc, axis=-1).astype(v.dtype)
        return jnp.einsum('bhqk,bkhd->bqhd', p, v)

    o = lax.map(one, qb)
    return o.transpose(1, 0, 2, 3, 4).reshape(b, s, h * v.shape[-1])

def _mla_qkv(h, rope, w_in, q_norm_g, kv_norm_g, w_uq, w_ukv, with_queries):
    b, l, _ = h.shape
    z = h @ w_in
    c_q = z[..., :Q_LORA_RANK]
    c_kv = z[..., Q_LORA_RANK:Q_LORA_RANK + KV_LORA_RANK]
    k_rope = z[..., Q_LORA_RANK + KV_LORA_RANK:]
    kv = (_rmsnorm(c_kv, kv_norm_g) @ w_ukv).reshape(b, l, MLA_HEADS, QK_NOPE_DIM + V_HEAD_DIM)
    k_nope, v = kv[..., :QK_NOPE_DIM], kv[..., QK_NOPE_DIM:]
    if rope is not None:
        cos, sin = rope
        k_rope = _apply_rope(k_rope, cos, sin)
    k = jnp.concatenate([k_nope, jnp.broadcast_to(k_rope[:, :, None, :], (b, l, MLA_HEADS, QK_ROPE_DIM))], axis=-1)
    if not with_queries:
        return None, k, v
    q = (_rmsnorm(c_q, q_norm_g) @ w_uq).reshape(b, l, MLA_HEADS, QK_NOPE_DIM + QK_ROPE_DIM)
    q_nope, q_rope = q[..., :QK_NOPE_DIM], q[..., QK_NOPE_DIM:]
    if rope is not None:
        q_rope = _apply_rope(q_rope, cos[:, None, :], sin[:, None, :])
    return jnp.concatenate([q_nope, q_rope], axis=-1), k, v

def _centred_mean_minus_self(x, window):
    b, l, ch = x.shape
    xf = x.astype(jnp.float32)
    cs = jnp.concatenate([jnp.zeros((b, 1, ch), jnp.float32), jnp.cumsum(xf, axis=1)], axis=1)
    t = jnp.arange(l)
    lo = jnp.clip(t - window // 2, 0, l)
    hi = jnp.clip(t + window // 2, 0, l)
    tot = jnp.take(cs, hi, axis=1) - jnp.take(cs, lo, axis=1)
    cnt = (hi - lo).astype(jnp.float32)[None, :, None]
    return (tot / cnt - xf).astype(x.dtype)

def _pool_mixer(h, w_in, w_grp, scale, w_out):
    b, l, _ = h.shape
    zg = (h @ w_in).reshape(b, l, N_POOL_GROUPS, POOL_GROUP_DIM)
    pooled = jnp.stack([_centred_mean_minus_self(zg[:, :, g], POOL_WINDOWS[g]) for g in range(N_POOL_GROUPS)], axis=2)
    y = jnp.einsum('blgc,gcd->blgd', pooled, w_grp).reshape(b, l, D_MODEL) * scale
    return y @ w_out

def _peer(h, w_q, k1, k2, u_tab, v_tab):
    b, l, d = h.shape
    q = (h @ w_q).reshape(b, l, PEER_HEADS, 2, PEER_HALF)
    s1 = jnp.einsum('blhc,hnc->blhn', q[..., 0, :], k1, preferred_element_type=jnp.float32)
    s2 = jnp.einsum('blhc,hnc->blhn', q[..., 1, :], k2, preferred_element_type=jnp.float32)
    v1, i1 = lax.top_k(s1, PEER_TOPK)
    v2, i2 = lax.top_k(s2, PEER_TOPK)
    cand_s = (v1[..., :, None] + v2[..., None, :]).reshape(b, l, PEER_HEADS, PEER_TOPK * PEER_TOPK)
    cand_i = (i1[..., :, None] * PEER_N_KEYS + i2[..., None, :]).reshape(b, l, PEER_HEADS, PEER_TOPK * PEER_TOPK)
    top_s, pos = lax.top_k(cand_s, PEER_TOPK)
    idx = jnp.take_along_axis(cand_i, pos, axis=-1)
    g = jax.nn.softmax(top_s, axis=-1).astype(h.dtype)
    n_blk = (b * l) // PEER_BLOCK
    n_sel = PEER_HEADS * PEER_TOPK
    hb = h.reshape(n_blk, PEER_BLOCK, d)
    ib = idx.reshape(n_blk, PEER_BLOCK, n_sel)
    gb = g.reshape(n_blk, PEER_BLOCK, n_sel)

    def one(args):
        hx, ix, gx = args
        u = jnp.take(u_tab, ix, axis=0)
        a = jax.nn.gelu(jnp.einsum('ted,td->te', u, hx), approximate=False)
        vv = jnp.take(v_tab, ix, axis=0)
        return jnp.einsum('te,ted->td', gx * a, vv)

    return lax.map(one, (hb, ib, gb)).reshape(b, l, d)

def _post_norm(x, y, gate, g, b):
    return _layernorm(DEEPNORM_ALPHA * x + gate * y, g, b)

def second_inputs(seed: int = 0) -> dict:
    key = jax.random.key(seed)
    ks = jax.random.split(key, 24)
    nrm = lambda k, shp, s: jax.random.normal(k, shp, jnp.float32) * s
    D = D_MODEL
    return {
        "x": nrm(ks[0], (BATCH, SEQ, D), 1.0),
        "c": nrm(ks[1], (BATCH, D), 1.0),
        "ctx": nrm(ks[2], (BATCH, CTX_LEN, D), 1.0),
        "c_ctx": nrm(ks[3], (D,), 1.0),
        "w_mod": nrm(ks[4], (DEPTH, D, N_MOD * D), 0.5 * D ** -0.5),
        "b_mod": nrm(ks[5], (DEPTH, N_MOD * D), 0.02),
        "ln_g": 1.0 + nrm(ks[6], (DEPTH, 2, D), 0.05),
        "ln_b": nrm(ks[7], (DEPTH, 2, D), 0.02),
        "mla_w_in": nrm(ks[8], (N_MLA_LAYERS, D, MLA_IN_DIM), D ** -0.5),
        "mla_q_norm": 1.0 + nrm(ks[9], (N_MLA_LAYERS, Q_LORA_RANK), 0.05),
        "mla_kv_norm": 1.0 + nrm(ks[10], (N_MLA_LAYERS, KV_LORA_RANK), 0.05),
        "mla_w_uq": nrm(ks[11], (N_MLA_LAYERS, Q_LORA_RANK, MLA_HEADS * (QK_NOPE_DIM + QK_ROPE_DIM)), Q_LORA_RANK ** -0.5),
        "mla_w_ukv": nrm(ks[12], (N_MLA_LAYERS, KV_LORA_RANK, MLA_HEADS * (QK_NOPE_DIM + V_HEAD_DIM)), KV_LORA_RANK ** -0.5),
        "mla_w_o": nrm(ks[13], (N_MLA_LAYERS, MLA_HEADS * V_HEAD_DIM, D), DEEPNORM_BETA * (MLA_HEADS * V_HEAD_DIM) ** -0.5),
        "pool_w_in": nrm(ks[14], (N_POOL_LAYERS, D, D), D ** -0.5),
        "pool_w_grp": nrm(ks[15], (N_POOL_LAYERS, N_POOL_GROUPS, POOL_GROUP_DIM, POOL_GROUP_DIM), POOL_GROUP_DIM ** -0.5),
        "pool_scale": 1.0 + nrm(ks[16], (N_POOL_LAYERS, D), 0.1),
        "pool_w_out": nrm(ks[17], (N_POOL_LAYERS, D, D), DEEPNORM_BETA * D ** -0.5),
        "peer_w_q": nrm(ks[18], (DEPTH, D, PEER_HEADS * PEER_QUERY_DIM), D ** -0.5),
        "peer_k1": nrm(ks[19], (DEPTH, PEER_HEADS, PEER_N_KEYS, PEER_HALF), PEER_HALF ** -0.5),
        "peer_k2": nrm(ks[20], (DEPTH, PEER_HEADS, PEER_N_KEYS, PEER_HALF), PEER_HALF ** -0.5),
        "peer_u": nrm(ks[21], (DEPTH, PEER_N_EXPERTS, D), D ** -0.5),
        "peer_v": nrm(ks[22], (DEPTH, PEER_N_EXPERTS, D), DEEPNORM_BETA),
    }

def second_block(x, c, ctx, c_ctx, w_mod, b_mod, ln_g, ln_b, mla_w_in, mla_q_norm, mla_kv_norm, mla_w_uq, mla_w_ukv, mla_w_o,
              pool_w_in, pool_w_grp, pool_scale, pool_w_out, peer_w_q, peer_k1, peer_k2, peer_u, peer_v):
    b, s, _ = x.shape
    rope = _axial_rope_tables(s)
    silu_c = jax.nn.silu(c)
    silu_ctx = jax.nn.silu(c_ctx)
    for i in range(DEPTH):
        mixer = i % N_MIXERS
        j = i // N_MIXERS
        ctx_needed = any(k % N_MIXERS == 0 for k in range(i + 1, DEPTH))
        ml = (silu_c @ w_mod[i] + b_mod[i])[:, None, :]
        mc = silu_ctx @ w_mod[i] + b_mod[i]
        sh1, sc1, g1, sh2, sc2, g2 = jnp.split(ml, N_MOD, axis=-1)
        csh1, csc1, cg1, csh2, csc2, cg2 = jnp.split(mc, N_MOD, axis=-1)
        hx = x * (1.0 + sc1) + sh1
        hc = ctx * (1.0 + csc1) + csh1
        if mixer == 0:
            w = (mla_w_in[j], mla_q_norm[j], mla_kv_norm[j], mla_w_uq[j], mla_w_ukv[j])
            q, k, v = _mla_qkv(hx, rope, *w, True)
            qc, kc, vc = _mla_qkv(hc, None, *w, ctx_needed)
            y = _block_attention(q, jnp.concatenate([k, kc], axis=1), jnp.concatenate([v, vc], axis=1)) @ mla_w_o[j]
            if ctx_needed:
                yc = _block_attention(qc, kc, vc) @ mla_w_o[j]
        else:
            w = (pool_w_in[j], pool_w_grp[j], pool_scale[j], pool_w_out[j])
            y = _pool_mixer(hx, *w)
            if ctx_needed:
                yc = _pool_mixer(hc, *w)
        pw = (peer_w_q[i], peer_k1[i], peer_k2[i], peer_u[i], peer_v[i])
        x = _post_norm(x, y, g1, ln_g[i, 0], ln_b[i, 0])
        x = _post_norm(x, _peer(x * (1.0 + sc2) + sh2, *pw), g2, ln_g[i, 1], ln_b[i, 1])
        if ctx_needed:
            ctx = _post_norm(ctx, yc, cg1, ln_g[i, 0], ln_b[i, 0])
            ctx = _post_norm(ctx, _peer(ctx * (1.0 + csc2) + csh2, *pw), cg2, ln_g[i, 1], ln_b[i, 1])
    return x


def setup_inputs(seed=0):
    out = dict(first_inputs(seed))
    for name, value in second_inputs(seed + 1).items():
        if name != "x":
            out[name + "_2"] = value
    return out


def reference(
    x, w_in, w_out, pre_mix_w, post_mix_w, pre_mlp_w, post_mlp_w, w_ff1, w_ff2, conv_dw_w,
    conv_dw_b, conv_ln_w, conv_ln_b, diff_lambda_q1, diff_lambda_k1, diff_lambda_q2,
    diff_lambda_k2, diff_subln_w, delta_conv_w, delta_A_log, delta_dt_bias, delta_norm_w, c_2,
    ctx_2, c_ctx_2, w_mod_2, b_mod_2, ln_g_2, ln_b_2, mla_w_in_2, mla_q_norm_2, mla_kv_norm_2,
    mla_w_uq_2, mla_w_ukv_2, mla_w_o_2, pool_w_in_2, pool_w_grp_2, pool_scale_2, pool_w_out_2,
    peer_w_q_2, peer_k1_2, peer_k2_2, peer_u_2, peer_v_2,
):
    x = first_block(
        x, w_in, w_out, pre_mix_w, post_mix_w, pre_mlp_w, post_mlp_w, w_ff1, w_ff2, conv_dw_w,
        conv_dw_b, conv_ln_w, conv_ln_b, diff_lambda_q1, diff_lambda_k1, diff_lambda_q2,
        diff_lambda_k2, diff_subln_w, delta_conv_w, delta_A_log, delta_dt_bias, delta_norm_w,
    )
    return second_block(
        x, c_2, ctx_2, c_ctx_2, w_mod_2, b_mod_2, ln_g_2, ln_b_2, mla_w_in_2, mla_q_norm_2,
        mla_kv_norm_2, mla_w_uq_2, mla_w_ukv_2, mla_w_o_2, pool_w_in_2, pool_w_grp_2,
        pool_scale_2, pool_w_out_2, peer_w_q_2, peer_k1_2, peer_k2_2, peer_u_2, peer_v_2,
    )


_drawn_inputs = setup_inputs


def setup_inputs(seed=0):
    import zlib

    import numpy as np

    out = dict(_drawn_inputs(seed))
    spreads = {}
    factors = {'conv_ln_b': 4.242,
     'ctx_2': 8.0,
     'c_ctx_2': 6.676,
     'b_mod_2': 3.368,
     'mla_w_in_2': 2.962,
     'mla_q_norm_2': 8.0,
     'mla_kv_norm_2': 8.0,
     'mla_w_uq_2': 5.65,
     'mla_w_ukv_2': 2.893,
     'mla_w_o_2': 2.788,
     'pool_scale_2': 5.185}
    for name, (base, spread) in spreads.items():
        noise = np.random.default_rng([zlib.crc32(name.encode()), seed]).standard_normal(out[name].shape)
        drawn = base * np.exp(spread * noise) if base else spread * noise
        out[name] = jnp.asarray(drawn.astype(out[name].dtype))
    for name, factor in factors.items():
        out[name] = (out[name] * factor).astype(out[name].dtype)
    return out
```

```python
from contextlib import ExitStack
import math

import numpy as np

import concourse.bass as bass
from concourse import mybir

F32 = mybir.dt.float32
F32R = mybir.dt.float32r
U32 = mybir.dt.uint32
BF16 = mybir.dt.bfloat16
ALU = mybir.AluOpType
ACT = mybir.ActivationFunctionType
AX = mybir.AxisListType

P = 128
S = 256
TB = S // P
D = 1024
KT = D // P
DEPTH = 2
HD = 64
CONV_CH, CONV_W = 256, 31
PADC = CONV_W // 2
DH, NMAP, DD = 6, 12, 32
GH = 6
PAIRS = GH // 2
CHUNK = 64
MATS = 2 * GH * TB
GRP = MATS // PAIRS
F_FF = 4096
RING = 4
SLOT = 2048
SPLIT = KT * S + 4 * D
BANK = 512
NBANK = 4
CTX = 256
MH, NOPE, ROPE, VD = 8, 128, 64, 128
QR, KVR = 384, 256
NK = 128
PH, TOPK = 8, 16
HH = 2 * PH
WINDOWS = (2, 4, 8, 16)
ALPHA = (2.0 * DEPTH) ** 0.25
NEG = -3.4e38

MIX_SLOTS, FF_SLOTS = 4 + 10 + 4, F_FF // P
LAYER_SLOTS = MIX_SLOTS + FF_SLOTS
MOD_SLOTS, MLA_SLOTS, QK_SLOTS, EXP_SLOTS, POOL_SLOTS = 48, 12, 9, 128, 9


class Stream:

    def __init__(self):
        self.base, self.before, self.prior = {}, {}, {}
        g, loads, last = 0, [0] * RING, [None] * RING
        order = []
        for _ in range(DEPTH):
            order += [("mix", MIX_SLOTS), ("ff", FF_SLOTS)]
        order += [("mod", MOD_SLOTS), ("mla", MLA_SLOTS), ("qk0", QK_SLOTS), ("exp0", EXP_SLOTS),
                  ("pool", POOL_SLOTS), ("qk1", QK_SLOTS), ("exp1", EXP_SLOTS)]
        self.order = order
        seen = {}
        for seg, n in order:
            rep = seen.get(seg, 0)
            seen[seg] = rep + 1
            if rep == 0:
                self.base[seg], self.before[seg] = g, list(loads)
            if rep == 1:
                self.per_layer = [a - b for a, b in zip(loads, self.before[seg])] if seg == "mix" else self.per_layer
            for pos in range(n):
                r = pos % RING
                if pos < RING:
                    self.prior[(seg, rep, pos)] = last[r]
                last[r] = g
                loads[r] += 1
                g += 1

    def loaded(self, seg, pos, lay=None):
        r = pos % RING
        n = 16 * (self.before[seg][r] + pos // RING + 1)
        return n if lay is None else lay * (16 * self.per_layer[r]) + n

    def used(self, seg, pos, lay=None):
        n = self.base[seg] + pos + 1
        return n if lay is None else lay * LAYER_SLOTS + n


STREAM = Stream()


class Jobs:

    def __init__(self, jobs):
        self.n = len(jobs)
        self.at, self.who, self.nth = {}, [], []
        total = {"act": 0, "dve": 0}
        for i, (key, who) in enumerate(jobs):
            assert key not in self.at, key
            self.at[key] = i
            total[who] += 1
            self.who.append(who)
            self.nth.append(total[who])
        self.total = total

    def sems(self, ctx, nc, name):
        self.filled = ctx.enter_context(nc.semaphore(f"{name}_bank_filled"))
        self.read = {w: ctx.enter_context(nc.semaphore(f"{name}_bank_read_{w}")) for w in ("act", "dve")}
        self.next = {"pe": 0, "act": 0, "dve": 0}
        return self

    def _at(self, it, per, n):
        return n if it is None else it * per + n

    def give(self, pe, key, it=None):
        i = self.at[key]
        assert i == self.next["pe"] % self.n, (key, i, self.next["pe"])
        self.next["pe"] += 1
        if i >= NBANK:
            w = self.who[i - NBANK]
            pe.wait_ge(self.read[w], self._at(it, self.total[w], self.nth[i - NBANK]))
        return i % NBANK

    def take(self, eng, who, key, it=None):
        i = self.at[key]
        assert self.who[i] == who and self.nth[i] - 1 == self.next[who] % self.total[who], (key, who)
        self.next[who] += 1
        eng.wait_ge(self.filled, self._at(it, self.n, i + 1))
        return i % NBANK

    def evac(self, eng, key, it=None):
        i = self.at[key]
        w = self.who[i]
        eng.wait_ge(self.read[w], self._at(it, self.total[w], self.nth[i]))

    def peek(self, eng, key, it=None):
        i = self.at[key]
        eng.wait_ge(self.filled, self._at(it, self.n, i + 1))
        return i % NBANK


def groups():
    return [(dr, hp, tb) for dr in range(2) for hp in range(2) for tb in range(TB)]


def layer_jobs():
    j = [(("h", i), "act" if i % 2 == 0 else "dve") for i in range(4)]
    j += [(("zb", tb), "act") for tb in range(TB)] + [(("dv", tb), "act") for tb in range(TB)]
    j += [(("s", i), "act") for i in range(5)]
    j += [("cg", "act"), ("ca", "dve")] + [(("d", i), "act") for i in range(3)]
    j += [("gc", "dve"), ("gl", "act")]
    j += [(("l2", i), "act") for i in range(3)]
    j += [(("sc", m), "dve") for m in range(NMAP)]
    for h in range(DH + 1):
        j += [(("ar", h), "act")] * (h < DH) + [(("av", h - 1), "act")] * (h > 0)
    j += [(("yd", i), "act") for i in range(2)]
    j += [(("gr", g), "dve") for g in range(GRP)]
    j += [(("kn", tb), "act") for tb in range(TB)] + [(("vn", tb), "act") for tb in range(TB)]
    for hp in range(2):
        for tb in range(TB):
            j += [(("kk", hp, tb), "dve"), (("qk", hp, tb), "dve")]
    for g in range(GRP):
        j += [(("at", g), "act"), (("qt", g), "act")]
    j += [(("d2", g), "act") for g in range(GRP)] + [(("d2t", g), "act") for g in range(GRP)]
    j += [(("p1", g), "dve") for g in range(GRP)] + [(("p1t", g), "dve") for g in range(GRP)]
    j += [(("d4", g), "act") for g in range(GRP)] + [(("d4t", g), "act") for g in range(GRP)]
    j += [(("t8", g), "dve") for g in range(GRP)] + [(("t8t", g), "dve") for g in range(GRP)]
    for b in range(3):
        j += [(("y", b, g), "act") for g in range(GRP)]
        for g in range(GRP):
            j += [(("ty", b, g), "dve")] * (b < 2) + [(("tyt", b, g), "dve")]
    j += [(("w", dr, tb), "act") for dr in range(2) for tb in range(TB)]
    for n in range(4):
        j += [(("v", n), "dve")] + [(("qs", n), "dve")] * (n > 0)
        j += [(("kv", n, dr), "dve") for dr in range(2)] * (n < 3) + [(("ao", n), "dve")]
    j += [("cm", "dve"), ("cv", "act")]
    j += [(("yx", i), "act") for i in range(2)]
    j += [(("h2", i), "act" if i % 2 == 0 else "dve") for i in range(4)]
    return j


class Sig:

    def __init__(self, ctx, nc, name, per):
        self.sem, self.per, self.name = ctx.enter_context(nc.semaphore(name)), per, name

    def at(self, n=None, it=None):
        n = self.per if n is None else n
        assert 0 < n <= self.per, (self.name, n)
        return n if it is None else it * self.per + n


class Steps:

    def __init__(self, eng, sem, per, it=None):
        self.eng, self.sem, self.per, self.it, self.n = eng, sem, per, it, 0

    def done(self, ins):
        ins.then_inc(self.sem, 1)
        self.n += 1

    def settle(self):
        self.eng.wait_ge(self.sem, self.n if self.it is None else self.it * self.per + self.n)

    def link(self, ins):
        self.done(ins)
        self.settle()

    def close(self, name):
        assert self.n == self.per, f"{name}: {self.n} steps, not {self.per}"


class Arena:

    def __init__(self, t, off=0):
        self.t, self.off = t, off

    def take(self, *dims):
        n = math.prod(dims)
        v = self.t[:, self.off:self.off + n]
        self.off += n
        assert self.off <= self.t.shape[1], (self.off, self.t.shape)
        return shaped(v, *dims)


def shaped(v, *dims):
    if len(dims) == 1:
        return v
    names = "abcd"[:len(dims)]
    return v.rearrange(f"p ({' '.join(names)}) -> p {' '.join(names)}", **{k: d for k, d in zip(names[1:], dims[1:])})


MATRICES = ("ident", "ones", "iota", "tri_f", "tri_b", "same", "pen_f", "pen_b", "notdiag", "bd8", "m8", "m16", "m32", "rot")
COLUMNS = (-0.5, 1e-6, 1e-5, 1.0 / D, 1.0 / HD)
C_COL = 3 * P
C_LATE = C_COL + len(COLUMNS)
C_DIST = C_LATE + (len(MATRICES) - 3) * P
C_COS = C_DIST + TB * S
C_SIN = C_COS + S
C_POOL = C_SIN + S
CONST = C_POOL + len(WINDOWS) * S


def constants():
    i, j = np.arange(P)[:, None], np.arange(P)[None, :]
    same = i // CHUNK == j // CHUNK
    mats = {
        "ident": i == j,
        "tri_f": same & (i <= j),
        "tri_b": same & (i >= j),
        "same": same,
        "ones": i + j >= 0,
        "pen_f": np.where(same & (i >= j), 0.0, 1e30),
        "pen_b": np.where(same & (i <= j), 0.0, 1e30),
        "notdiag": i != j,
        "bd8": i // 8 == j // 8,
        "m8": (i // 8 != j // 8) & (i // 16 == j // 16),
        "m16": (i // 16 != j // 16) & (i // 32 == j // 32),
        "m32": (i // 32 != j // 32) & (i // 64 == j // 64),
        "iota": 0 * i + j,
    }
    half = ROPE // 2
    rot = np.zeros((P, P))
    for b in range(0, P, ROPE):
        for a in range(half):
            rot[b + half + a, b + a] = -1.0
            rot[b + a, b + half + a] = 1.0
    mats["rot"] = rot
    q = np.arange(S).reshape(TB, P)
    dist = np.abs(q.T[:, :, None] - np.arange(S)[None, None, :]).reshape(P, TB * S)
    grid = 64
    rows = S // grid
    row = np.repeat(np.arange(rows), grid).astype(np.float32)
    col = np.tile(np.arange(grid), rows).astype(np.float32)
    freqs = (np.float32(10000.0) ** (-np.arange(ROPE // 4, dtype=np.float32) / np.float32(ROPE // 4))).astype(np.float32)
    ang = np.concatenate([row[:, None] * freqs, col[:, None] * freqs], -1)
    cols = np.tile(np.array([COLUMNS]), (P, 1))
    t = np.arange(S)
    cnt = [np.tile(1.0 / (np.clip(t + w // 2, 0, S) - np.clip(t - w // 2, 0, S))[None, :], (P, 1)) for w in WINDOWS]
    out = [mats[m] for m in MATRICES[:3]] + [cols] + [mats[m] for m in MATRICES[3:]]
    out += [dist, np.tile(np.cos(ang).T, (4, 1)), np.tile(np.sin(ang).T, (4, 1))] + cnt
    return np.concatenate([np.asarray(a, np.float32) for a in out], 1)


def alibi(n):
    c = 2 ** int(math.floor(math.log2(n)))
    pow2 = lambda m: [(2.0 ** (-8.0 / m)) ** (i + 1) for i in range(m)]
    return pow2(n) if c == n else pow2(c) + pow2(2 * c)[0::2][:n - c]


V_PRE, V_MLP, V_TAP, V_CB, V_LNW, V_LNB, V_SUB, V_DN, V_DT = 0, 8, 16, 78, 80, 82, 84, 85, 86
VCOLS = V_DT + 27
R_LAM, R_ALOG, R_DTB, R_INIT = 0, 128, 140, 152
RCOLS = 153

DVE_STEPS, POOL_STEPS, ACT_STEPS = 185, 86, 10


class Ctx:
    pass


def plan_memory(nc, ctx, k):
    start = -(-nc.sbuf_base // 32) * 32
    ring = ctx.enter_context(nc.sbuf_tensor("ring", [P, RING * SLOT], F32))
    k.sb = ctx.enter_context(nc.sbuf_tensor("sb", [P, 53200 - RING * SLOT], F32))
    k.alias = lambda name, at, n: nc.alloc_sbuf_tensor_at(name, [P, n], F32R, offset=start + 4 * (RING * SLOT + at), align_bytes=4)
    k.psum = [ctx.enter_context(nc.psum_tensor(f"bank{i}", [P, BANK], F32)) for i in range(8)]
    a = Arena(k.sb)
    k.ring = [ring[:, i * SLOT:(i + 1) * SLOT] for i in range(RING)]
    ring_r = k.alias("ring_r", -RING * SLOT, RING * SLOT)
    k.ring_r = [ring_r[:, i * SLOT:(i + 1) * SLOT] for i in range(RING)]
    k.x = a.take(TB, D)
    k.hT_r = shaped(k.alias("hT_r", a.off, KT * S)[:, :], KT, S)
    k.hT = a.take(KT, S)
    k.stat = a.take(16)
    k.zero = a.take(64).bitcast(BF16)
    k.zero_row = a.take(256).bitcast(BF16)
    k.const = a.take(C_POOL)
    k.c = {m: k.const[:, i * P:(i + 1) * P] if i < 3 else k.const[:, C_LATE + (i - 3) * P:C_LATE + (i - 2) * P]
           for i, m in enumerate(MATRICES)}
    k.dist = shaped(k.const[:, C_DIST:C_COS], TB, S)
    k.cos, k.sin = k.const[:, C_COS:C_SIN], k.const[:, C_SIN:C_POOL]
    k.minus_half, k.eps6, k.eps5, k.inv_d, k.inv_hd = (k.const[:, C_COL + i:C_COL + i + 1] for i in range(5))
    k.free = a.off
    k.late = k.free - (C_POOL - C_LATE)
    b = Arena(k.sb, k.free)
    k.B = [b.take(MATS, P) for _ in range(8)]
    flat = [m.rearrange("p a b -> p (a b)") for m in k.B]
    k.E, k.ES, k.A, k.AQ, k.DT, k.D2T, k.T, k.TT = k.B
    k.AT, k.AQT, k.DM, k.D2, k.Y = k.B[0], k.B[1], k.B[2], k.B[3], k.B[3]
    k.D4, k.D4T, k.LT = k.B[2], k.B[4], k.B[2]
    k.prob = k.sb[:, k.free:k.free + NMAP * TB * S].rearrange("p (m q k) -> p m q k", m=NMAP, q=TB)
    k.ATd = [shaped(flat[2][:, i * 512:(i + 1) * 512], TB, S) for i in range(2)]
    k.qkd = shaped(flat[2][:, 1024:1024 + 1536], 6, S)
    k.od = shaped(flat[3][:, 0:768], TB, 384)
    k.dv = shaped(flat[3][:, 768:1536], TB, 384)
    k.od2 = shaped(flat[3][:, 1536:2304], TB, 384)
    k.raw = shaped(flat[4][:, 0:9 * 258], 9, 258)
    k.sq = shaped(flat[5][:, 0:1536], 6, S)
    k.rn = shaped(flat[5][:, 1536:3072], 6, S)
    k.post = [flat[5][:, i * D:(i + 1) * D] for i in range(2)]
    k.xn = shaped(flat[6][:, 0:2048], TB, D)
    k.csig = shaped(flat[6][:, 2048:2560], 2, S)
    k.nwT = shaped(flat[6][:, 0:1536], 2, TB, PAIRS, P)
    k.junk = flat[7][:, 0:1024]
    k.tmp512 = [flat[7][:, 1024:1536], flat[7][:, 1536:2048]]
    k.ff_at = k.free
    k.ff_hi = k.free + MATS * P
    k.cxc = shaped(flat[0][:, 0:512], 2, S)
    k.csq = shaped(flat[0][:, 512:1024], 2, S)
    k.crs = flat[0][:, 1024:1280]
    k.o2 = shaped(flat[0][:, 1536:2304], TB, 384)
    k.sT = b.take(9, S)
    k.zs = b.take(TB, 384)
    k.Kn, k.Vn = b.take(TB, 384), b.take(TB, 384)
    k.o = k.Kn
    k.kbg, k.kdec, k.vb = b.take(2, TB, 384), b.take(2, TB, 384), b.take(2, TB, 384)
    k.st = b.take(2, PAIRS, P)
    scan = b.take(768)
    k.qse, k.v = scan[:, 0:384], scan[:, 384:768]
    k.cpad = shaped(scan[:, 0:2 * (S + 2 * PADC)], 2, S + 2 * PADC)
    k.cacc = b.take(2, S)
    k.ctap = k.hT[:, 0:2, :]
    k.ba = b.take(TB, 24)
    k.ga = b.take(TB, GH * 2)
    k.gb = b.take(TB, GH * 2)
    k.ge = b.take(TB, GH * 2)
    k.g = b.take(TB, GH * 2)
    k.beta = b.take(TB, GH * 2)
    k.gsum_c = b.take(TB, 24)
    k.eg = b.take(TB, GH * 2)
    k.ekd = b.take(TB, GH * 2)
    k.beg = b.take(TB, GH * 2)
    k.gl = b.take(4, 6)
    k.mx = b.take(NMAP, TB)
    k.ssum = b.take(NMAP, TB)
    k.negA = b.take(12)
    k.lam = b.take(8)
    k.lprod = b.take(2, 32)
    k.sub = b.take(1)
    k.onorm = b.take(12)
    k.vec = b.take(VCOLS)
    k.row = b.take(RCOLS)
    k.block1_end = b.off


def group_cols(v, tb, dr, hp):
    return v[:, tb, dr * GH + hp:dr * GH + hp + 5:2]


class Release:

    def __init__(self, k):
        self.k, self.owed = k, 0

    def owe(self):
        self.owed += 1

    def pay(self, ins):
        if self.owed:
            ins.then_inc(self.k.weights_used, self.owed)
            self.owed = 0


def slot(k, pe, seg, pos, lay=None):
    pe.wait_ge(k.weights_loaded[pos % RING], STREAM.loaded(seg, pos, lay))
    return k.ring[pos % RING]


def pe_transpose_x(k, pe, J, key, src, lay, rel=None):
    for i in range(4):
        b = J.give(pe, (key, i), lay)
        for kk in range(2):
            for tb in range(TB):
                t = pe.transpose(k.psum[b][:, kk * S + tb * P:kk * S + (tb + 1) * P],
                                 src[:, tb, (2 * i + kk) * P:(2 * i + kk + 1) * P], k.c["ident"])
                if rel is not None and tb == 0 and kk == 0:
                    rel.pay(t)
        t.then_inc(J.filled, 1)


def pe_layer(k, pe, lay):
    J, c, ps, rel = k.J1, k.c, k.psum, Release(k)
    wait = lambda sig, n=None: pe.wait_ge(sig.sem, sig.at(n, lay))
    wait(k.h_scaled, 2)
    pe_transpose_x(k, pe, J, "h", k.xn, lay)
    J.evac(pe, ("h", 2), lay)
    J.evac(pe, ("h", 3), lay)
    slots = [slot(k, pe, "mix", s, lay) for s in range(4)]
    for name, c0, n in (("zb", 0, 408), ("dv", 408, 384)):
        for tb in range(TB):
            b = J.give(pe, (name, tb), lay)
            for kt in range(KT):
                m = pe.matmul(ps[b][:, 0:n], k.hT[:, kt, tb * P:(tb + 1) * P],
                              slots[kt // 2][:, (kt % 2) * 792 + c0:(kt % 2) * 792 + c0 + n],
                              start=kt == 0, stop=kt == KT - 1)
                if name == "dv" and tb == 1 and kt in (1, 3, 5):
                    m.then_inc(k.weights_used, 1)
            m.then_inc(J.filled, 1)
    rel.owe()
    for i, key in enumerate([("s", j) for j in range(5)] + ["cg", "ca"] + [("d", j) for j in range(3)]):
        w = slot(k, pe, "mix", 4 + i, lay)
        b = J.give(pe, key, lay)
        for half in range(1 if key == ("s", 4) else 2):
            for kt in range(KT):
                m = pe.matmul(ps[b][:, half * S:(half + 1) * S], w[:, half * 1024 + kt * P:half * 1024 + (kt + 1) * P],
                              k.hT[:, kt, :], start=kt == 0, stop=kt == KT - 1)
                if kt == 0:
                    rel.pay(m)
        m.then_inc(J.filled, 1)
        rel.owe()
    wait(k.g_ready)
    b = J.give(pe, "gc", lay)
    for tb in range(TB):
        rel.pay(pe.matmul(ps[b][:, tb * 24:tb * 24 + 6], c["tri_f"], k.g[:, tb, 0:6], start=True, stop=True))
        pe.matmul(ps[b][:, tb * 24 + 6:tb * 24 + 12], c["tri_b"], k.g[:, tb, 6:12], start=True, stop=True)
        m = pe.matmul(ps[b][:, tb * 24 + 12:tb * 24 + 24], c["same"], k.g[:, tb, :], start=True, stop=True)
    m.then_inc(J.filled, 1)
    b = J.give(pe, "gl", lay)
    for hp in range(2):
        for ch in range(4):
            tb, par = ch // 2, ch % 2
            cols = k.g[:, tb, :].rearrange("p (d a h) -> p d a h", d=2, h=2)[:, :, :, hp]
            m = pe.matmul(ps[b][hp * 64:hp * 64 + 64, ch * 6:ch * 6 + 6], c["same"][:, par * 64:par * 64 + 64], cols,
                          start=True, stop=True)
    m.then_inc(J.filled, 1)
    wait(k.sq_ready)
    for i in range(3):
        b = J.give(pe, ("l2", i), lay)
        m = pe.matmul(ps[b][:, :], c["same"], k.sq[:, 2 * i:2 * i + 2, :], start=True, stop=True)
        m.then_inc(J.filled, 1)
    J.evac(pe, ("d", 2), lay)
    for m_ in range(NMAP):
        b = J.give(pe, ("sc", m_), lay)
        r = (m_ % 4) * DD
        for qb in range(TB):
            m = pe.matmul(ps[b][:, qb * S:(qb + 1) * S], k.qkd[r:r + DD, m_ // 4, qb * P:(qb + 1) * P],
                          k.qkd[r:r + DD, 3 + m_ // 4, :], start=True, stop=True)
        m.then_inc(J.filled, 1)

    def attend(h):
        J.evac(pe, ("ar", h), lay)
        b = J.give(pe, ("av", h), lay)
        for qb in range(TB):
            for kb in range(TB):
                m = pe.matmul(ps[b][:, qb * HD:(qb + 1) * HD], k.ATd[h % 2][:, kb, qb * P:(qb + 1) * P],
                              k.dv[:, kb, h * HD:(h + 1) * HD], start=kb == 0, stop=kb == TB - 1)
        m.then_inc(J.filled, 1)

    for h in range(DH):
        wait(k.attn_ready, h + 1)
        b = J.give(pe, ("ar", h), lay)
        for qb in range(TB):
            for kb in range(TB):
                m = pe.transpose(ps[b][:, kb * S + qb * P:kb * S + (qb + 1) * P],
                                 k.prob[:, 2 * h, qb, kb * P:(kb + 1) * P], c["ident"])
        m.then_inc(J.filled, 1)
        if h:
            attend(h - 1)
    attend(DH - 1)
    wait(k.od_ready)
    pe_transpose_heads(k, pe, J, "yd", k.od, lay)
    for g, (dr, hp, tb) in enumerate(groups()):
        b = J.give(pe, ("gr", g), lay)
        for p in range(PAIRS):
            m = pe.matmul(ps[b][:, p * P:(p + 1) * P], k.g[:, tb, dr * GH + 2 * p + hp:dr * GH + 2 * p + hp + 1].to_broadcast([P, P]),
                          c["tri_b" if dr else "tri_f"], start=True, stop=True)
        m.then_inc(J.filled, 1)
    wait(k.qk_normed)
    for name, base in (("kn", 3), ("vn", 6)):
        for tb in range(TB):
            b = J.give(pe, (name, tb), lay)
            for p in range(PAIRS):
                m = pe.transpose(ps[b][:, p * P:(p + 1) * P], k.sT[:, base + p, tb * P:(tb + 1) * P], c["ident"])
            m.then_inc(J.filled, 1)
    for hp in range(2):
        for tb in range(TB):
            for name, base in (("kk", 3), ("qk", 0)):
                b = J.give(pe, (name, hp, tb), lay)
                for p in range(PAIRS):
                    m = pe.matmul(ps[b][:, p * P:(p + 1) * P], k.sT[hp * HD:(hp + 1) * HD, base + p, tb * P:(tb + 1) * P],
                                  k.sT[hp * HD:(hp + 1) * HD, 3 + p, tb * P:(tb + 1) * P], start=True, stop=True)
                m.then_inc(J.filled, 1)
    for g in range(GRP):
        if g == 0:
            J.evac(pe, ("qk", 1, 1), lay)
        b = J.give(pe, ("at", g), lay)
        for p in range(PAIRS):
            m = pe.transpose(ps[b][:, p * P:(p + 1) * P], k.A[:, 3 * g + p, :], c["ident"])
        m.then_inc(J.filled, 1)
        b = J.give(pe, ("qt", g), lay)
        for p in range(PAIRS):
            m = pe.transpose(ps[b][:, p * P:(p + 1) * P], k.AQ[:, 3 * g + p, :], c["ident"])
        m.then_inc(J.filled, 1)

    def products(key, lhsT, rhs, g):
        b = J.give(pe, key, lay)
        for p in range(PAIRS):
            m = pe.matmul(ps[b][:, p * P:(p + 1) * P], lhsT[:, 3 * g + p, :], rhs[:, 3 * g + p, :], start=True, stop=True)
        m.then_inc(J.filled, 1)

    wait(k.D_ready)
    for g in range(GRP):
        products(("d2", g), k.DT, k.DM, g)
    for g in range(GRP):
        products(("d2t", g), k.DM, k.DT, g)
    wait(k.P0_ready)
    for g in range(GRP):
        if g == 0:
            J.evac(pe, ("d2", GRP - 1), lay)
            J.evac(pe, ("d2t", GRP - 1), lay)
        products(("p1", g), k.TT, k.D2, g)
    for g in range(GRP):
        products(("p1t", g), k.D2, k.TT, g)
    for g in range(GRP):
        products(("d4", g), k.D2T, k.D2, g)
    for g in range(GRP):
        products(("d4t", g), k.D2, k.D2T, g)
    for g in range(GRP):
        if g == 0:
            J.evac(pe, ("d4", GRP - 1), lay)
            J.evac(pe, ("d4t", GRP - 1), lay)
            J.evac(pe, ("p1t", GRP - 1), lay)
        products(("t8", g), k.TT, k.D4, g)
    for g in range(GRP):
        products(("t8t", g), k.D4, k.TT, g)
    for lv in range(3):
        for g in range(GRP):
            wait(k.LT_ready, lv * GRP + g + 1)
            products(("y", lv, g), k.LT, k.T, g)
        for g in range(GRP):
            J.evac(pe, ("y", lv, g), lay)
            if lv < 2:
                products(("ty", lv, g), k.TT, k.Y, g)
            products(("tyt", lv, g), k.Y, k.TT, g)
    J.evac(pe, ("tyt", 2, GRP - 1), lay)
    wait(k.kv_scaled)
    for dr in range(2):
        for tb in range(TB):
            b = J.give(pe, ("w", dr, tb), lay)
            for p in range(PAIRS):
                for hp in range(2):
                    g = groups().index((dr, hp, tb))
                    h = 2 * p + hp
                    m = pe.matmul(ps[b][hp * 64:hp * 64 + 64, p * P:(p + 1) * P], k.kbg[:, dr, tb, h * HD:(h + 1) * HD],
                                  k.TT[:, 3 * g + p, :], start=True, stop=True)
            m.then_inc(J.filled, 1)
    for n in range(4):
        where = [(n // 2, n % 2), (1 - n // 2, 1 - n % 2)]
        if n == 0:
            J.evac(pe, ("w", 1, 1), lay)
            wait(k.state_zeroed)
        else:
            J.evac(pe, ("kv", n - 1, 1), lay)
        b = J.give(pe, ("v", n), lay)
        for dr, (tb, par) in enumerate(where):
            rows = slice(par * 64, par * 64 + 64)
            for h in range(GH):
                g = groups().index((dr, h % 2, tb))
                m = pe.matmul(ps[b][rows, h * HD:(h + 1) * HD], k.TT[:, 3 * g + h // 2, rows],
                              k.vb[:, dr, tb, h * HD:(h + 1) * HD], start=h == 0, stop=False, skip_group_check=True)
            if n:
                for p in range(PAIRS):
                    m = pe.matmul(ps[b][rows, p * P:(p + 1) * P], k.nwT[:, dr, tb, p, rows], k.st[:, dr, p, :],
                                  start=False, stop=False, skip_group_check=True)
        m.then_inc(J.filled, 1)
        if n:
            b = J.give(pe, ("qs", n), lay)
            for dr, (tb, par) in enumerate(where):
                rows = slice(par * 64, par * 64 + 64)
                for p in range(PAIRS):
                    m = pe.matmul(ps[b][rows, p * P:(p + 1) * P], k.sT[:, p, tb * P + par * 64:tb * P + par * 64 + 64],
                                  k.st[:, dr, p, :], start=True, stop=True)
            m.then_inc(J.filled, 1)
        J.evac(pe, ("v", n), lay)
        if n < 3:
            for dr, (tb, par) in enumerate(where):
                rows = slice(par * 64, par * 64 + 64)
                b = J.give(pe, ("kv", n, dr), lay)
                for p in range(PAIRS):
                    m = pe.matmul(ps[b][:, p * P:(p + 1) * P], k.kdec[rows, dr, tb, p * P:(p + 1) * P],
                                  k.v[rows, p * P:(p + 1) * P], start=True, stop=True)
                m.then_inc(J.filled, 1)
        b = J.give(pe, ("ao", n), lay)
        for dr, (tb, par) in enumerate(where):
            rows = slice(par * 64, par * 64 + 64)
            for h in range(GH):
                g = groups().index((dr, h % 2, tb))
                m = pe.matmul(ps[b][rows, h * HD:(h + 1) * HD], k.AQT[:, 3 * g + h // 2, rows],
                              k.v[:, h * HD:(h + 1) * HD], start=True, stop=True)
        m.then_inc(J.filled, 1)
    wait(k.conv_done)
    b = J.give(pe, "cm", lay)
    for i in range(2):
        m = pe.matmul(ps[b][:, 0:S], c["ones"], k.cacc[:, i, :], start=i == 0, stop=i == 1)
    m.then_inc(J.filled, 1)
    wait(k.csq_ready)
    b = J.give(pe, "cv", lay)
    for i in range(2):
        m = pe.matmul(ps[b][:, 0:S], c["ones"], k.csq[:, i, :], start=i == 0, stop=i == 1)
    m.then_inc(J.filled, 1)
    wait(k.o_ready)
    pe_transpose_heads(k, pe, J, "yx", k.o, lay)
    wait(k.conv_out)
    J.evac(pe, ("yx", 1), lay)
    for s in range(4):
        w = slot(k, pe, "mix", 14 + s, lay)
        for kk in range(2):
            kt = 2 * s + kk
            for tb in range(TB):
                for half in range(2):
                    m = pe.matmul(ps[4 + 2 * tb + half][:, :], k.hT[:, kt, tb * P:(tb + 1) * P],
                                  w[:, kk * D + half * 512:kk * D + (half + 1) * 512], start=kt == 0, stop=kt == KT - 1)
        if s < 3:
            m.then_inc(k.weights_used, 1)
    m.then_inc(k.y_acc.sem, 1)
    rel.owe()
    wait(k.h_scaled, 4)
    pe_transpose_x(k, pe, J, "h2", k.xn, lay, rel)
    J.evac(pe, ("h2", 2), lay)
    J.evac(pe, ("h2", 3), lay)
    pe_experts(k, pe, FF_SLOTS, k.FF, lay, k.y_ff)


def pe_transpose_heads(k, pe, J, key, src, lay):
    for i in range(2):
        b = J.give(pe, (key, i), lay)
        for kk in range(2 if i == 0 else 1):
            for tb in range(TB):
                m = pe.transpose(k.psum[b][:, kk * S + tb * P:kk * S + (tb + 1) * P],
                                 src[:, tb, (2 * i + kk) * P:(2 * i + kk + 1) * P], k.c["ident"])
        m.then_inc(J.filled, 1)


def pe_experts(k, pe, n, X, lay, done):
    ps = k.psum
    base = X.base(lay)
    def up(u, j):
        pe.wait_ge(X.u_split, j)
        for kt in range(KT):
            hi, lo = X.uh[u % 2][:, kt * P:(kt + 1) * P], k.ring_r[u][:, kt * P:(kt + 1) * P]
            for i, (w, h) in enumerate(((hi, X.hh), (hi, k.hT_r), (lo, X.hh))):
                m = pe.matmul(ps[u][:, 0:S], w, h[:, kt, :], start=(kt, i) == (0, 0), stop=(kt, i) == (KT - 1, 2))
        m.then_inc(X.up, 1)

    def down(u, j):
        pe.wait_ge(X.v_split, j)
        pe.wait_ge(X.weighted, j)
        for tb in range(TB):
            t = slice(tb * P, (tb + 1) * P)
            for half in range(2):
                d = slice(half * 512, (half + 1) * 512)
                hi, lo = X.vh[u % 2][:, d], k.ring_r[u][:, D + half * 512:D + (half + 1) * 512]
                for g, w in ((X.gh[u % 2], hi), (X.gh[u % 2], lo), (X.gl[u % 2], hi)):
                    m = pe.matmul(ps[4 + 2 * tb + half][:, :], g[:, t], w, start=False, stop=False, skip_group_check=True)
        m.then_inc(k.weights_used, 1)

    for b in range(4):
        pe.matmul(ps[4 + b][:, :], k.zero[:, :], k.zero_row[:, :], start=True, stop=False, skip_group_check=True)
    pe.wait_ge(X.h_split, lay + 1)
    up(0, base + 1)
    with pe.Fori(0, n // 4 - 1) as i:
        for u in range(4):
            up((u + 1) % 4, base + i * 4 + (u + 2))
            down(u, base + i * 4 + (u + 1))
    for u in range(4):
        if u < 3:
            up(u + 1, base + (n - 4 + u + 2))
        down(u, base + (n - 4 + u + 1))
    pe.matmul(ps[7][:, 0:64], k.zero[:, :], k.zero_row[:, 0:64], start=False, stop=True,
              skip_group_check=True).then_inc(done.sem, 1)


def bc(v, *dims):
    return v.to_broadcast([P] + list(dims))


def dve_evac_h(k, v, J, key, col, lay):
    for i in (1, 3):
        b = J.take(v, "dve", (key, i), lay)
        for kk in range(2):
            kt = 2 * i + kk
            m = v.tensor_scalar(k.hT[:, kt, :], k.psum[b][:, kk * S:(kk + 1) * S], k.vec[:, col + kt:col + kt + 1], None, ALU.mult)
        m.then_inc(J.read["dve"], 1)


def dve_post(k, v, st, lay, which, done):
    v.wait_ge(k.y_rstd.sem, k.y_rstd.at(which + 1, lay))
    v.wait_ge(k.post_loaded, lay * 32 + 32)
    for tb in range(TB):
        for half in range(2):
            t = k.tmp512[half]
            st.link(v.scalar_tensor_tensor(t, k.psum[4 + 2 * tb + half][:, :], k.stat[:, 8 + tb:9 + tb],
                                           k.post[which][:, half * 512:(half + 1) * 512], ALU.mult, ALU.mult))
            m = v.tensor_tensor(k.x[:, tb, half * 512:(half + 1) * 512], k.x[:, tb, half * 512:(half + 1) * 512], t, ALU.add)
            if (tb, half) != (1, 1):
                st.link(m)
    m.then_inc(done.sem, 1)


def dve_experts(k, v, seg, n, X, lay, factor, static=False):
    base, chain0 = X.base(lay), lay * (4 * n + 1)
    slay = None if static else lay

    def high(dst, src, count):
        v.tensor_copy(dst, src).then_inc(X.chain, 1)
        v.wait_ge(X.chain, count)

    def split(hi, low, src, count, ready):
        high(hi, src, count)
        v.tensor_tensor(low, src, hi.bitcast(F32), ALU.subtract).then_inc(ready, 1)

    def u_split(u, more, j, count):
        v.wait_ge(k.weights_loaded[u], STREAM.loaded(seg, u, slay) + more)
        if j is not None:
            v.wait_ge(X.up, j)
        split(X.uh[u % 2], k.ring_r[u][:, 0:D], k.ring[u][:, 0:D], count, X.u_split)

    def v_split(u, used, count):
        if used is not None:
            v.wait_ge(k.weights_used, used)
        split(X.vh[u % 2], k.ring_r[u][:, D:SLOT], k.ring[u][:, D:SLOT], count, X.v_split)

    def weight(i, u, j, count):
        v.wait_ge(X.acted, j)
        v.tensor_tensor(X.g[u % 2], X.r[u % 2], factor(i, u), ALU.mult).then_inc(X.chain, 1)
        v.wait_ge(X.chain, count)
        split(X.gh[u % 2], X.gl[u % 2], X.g[u % 2], count + 1, X.weighted)

    split(X.hh, k.hT_r, k.hT, chain0 + 1, X.h_split)
    u_split(0, 0, None, chain0 + 2)
    v_split(0, None, chain0 + 3)
    u_split(1, 0, None, chain0 + 4)
    first = STREAM.used(seg, 0, slay) - 2

    def tile(i, u, last=False):
        count = chain0 + i * 16 + (4 * u + 4)
        if last and u == 3:
            count = count - 1
        weight(i, u, base + i * 4 + (u + 1), count + 1)
        ahead = not (last and u > 1)
        if ahead:
            u_split((u + 2) % 4, i * 16 + (16 if u > 1 else 0), base + i * 4 + (u + 1), count + 3)
        if not (last and u == 3):
            v_split((u + 1) % 4, first + i * 4 + (u + 1), count + (4 if ahead else 3))

    with v.Fori(0, n // 4 - 1) as i:
        for u in range(4):
            tile(i, u)
    for u in range(4):
        tile(n // 4 - 1, u, True)


def dve_layer(k, v, lay):
    J, c, ps = k.J1, k.c, k.psum
    st = Steps(v, k.dve_step, DVE_STEPS, lay)
    wait = lambda sig, n=None: v.wait_ge(sig.sem, sig.at(n, lay))
    v.wait_ge(k.params_loaded, lay * 32 + 32)
    wait(k.h_rstd, 1)
    for tb in range(TB):
        v.tensor_scalar(k.xn[:, tb, :], k.x[:, tb, :], k.stat[:, 8 + tb:9 + tb], None, ALU.mult).then_inc(k.h_scaled.sem, 1)
    st.done(v.memset(k.cpad[:, :, :], 0.0))
    st.done(v.memset(k.raw[:, :, 0:1], 0.0))
    st.done(v.memset(k.raw[:, :, S + 1:S + 2], 0.0))
    v.memset(k.st[:, :, :, :], 0.0).then_inc(k.state_zeroed.sem, 1)
    dve_evac_h(k, v, J, "h", V_PRE, lay)
    lamv = shaped(k.row[:, R_LAM:R_LAM + 128], 4, DD)
    st.link(v.tensor_tensor(k.lprod[:, :, :], lamv[:, 0:4:2, :], lamv[:, 1:4:2, :], ALU.mult))
    v.tensor_reduce(k.lam[:, 0:2], k.lprod[:, :, :], AX.X, ALU.add).then_inc(k.lam_arg.sem, 1)
    st.link(v.tensor_scalar(k.lam[:, 6:7], k.row[:, R_INIT:R_INIT + 1], -1.0, 1.0, ALU.mult, ALU.add))
    v.tensor_tensor(k.sub[:, :], k.vec[:, V_SUB:V_SUB + 1], k.lam[:, 6:7], ALU.mult).then_inc(k.sub_ready.sem, 1)
    J.evac(v, ("zb", 1), lay)
    st.link(v.tensor_tensor(k.ga[:, :, :], k.ba[:, :, 12:24], bc(k.row[:, R_DTB:R_DTB + 12].unsqueeze(1), TB, 12), ALU.add))
    st.link(v.tensor_scalar(k.gb[:, :, :], k.ga[:, :, :], -1.0, None, ALU.mult))
    v.tensor_tensor(k.gb[:, :, :], k.ga[:, :, :], k.gb[:, :, :], ALU.min).then_inc(k.gate_arg.sem, 1)
    wait(k.gate_exp)
    st.link(v.tensor_scalar(k.negA[:, :], k.negA[:, :], -1.0, None, ALU.mult))
    st.link(v.scalar_tensor_tensor(k.g[:, :, :], k.ga[:, :, :], 0.0, k.ge[:, :, :], ALU.max, ALU.add))
    v.tensor_tensor(k.g[:, :, :], k.g[:, :, :], bc(k.negA[:, :].unsqueeze(1), TB, 12), ALU.mult).then_inc(k.g_ready.sem, 1)
    st.link(v.tensor_scalar(k.beta[:, :, :], k.beta[:, :, :], 1.0, None, ALU.add))
    st.link(v.reciprocal(k.beta[:, :, :], k.beta[:, :, :]))
    J.evac(v, "cg", lay)
    b = J.take(v, "dve", "ca", lay)
    v.tensor_tensor(k.cpad[:, :, PADC:PADC + S], shaped(ps[b][:, :], 2, S), k.csig[:, :, :], ALU.mult).then_inc(J.read["dve"], 1)
    J.evac(v, ("s", 4), lay)
    for tap in range(3):
        for i in range(9):
            w = k.vec[:, V_DT + i * 3 + tap:V_DT + i * 3 + tap + 1]
            src = k.raw[:, i, tap:tap + S]
            if tap == 0:
                m = v.tensor_scalar(k.sT[:, i, :], src, w, None, ALU.mult)
            else:
                m = v.scalar_tensor_tensor(k.sT[:, i, :], src, w, k.sT[:, i, :], ALU.mult, ALU.add)
            if (tap, i) == (2, 8):
                m.then_inc(k.sconv.sem, 1)
            else:
                st.done(m)
        st.settle()
    b = J.take(v, "dve", "gc", lay)
    v.tensor_copy(k.gsum_c[:, :, :], shaped(ps[b][:, 0:48], TB, 24)).then_inc(J.read["dve"], 1)
    J.evac(v, "gc", lay)
    v.tensor_tensor(k.ekd[:, :, :], k.gsum_c[:, :, 12:24], k.gsum_c[:, :, 0:12], ALU.subtract).then_inc(k.gc_ready.sem, 1)
    wait(k.gc_exp)
    v.tensor_tensor(k.beg[:, :, :], k.beta[:, :, :], k.eg[:, :, :], ALU.mult).then_inc(k.beg_ready.sem, 1)
    J.evac(v, ("l2", 2), lay)
    st.link(v.reciprocal(k.rn[:, :, :], k.rn[:, :, :]))
    st.done(v.scalar_tensor_tensor(k.sT[:, 0:3, :], k.sT[:, 0:3, :], HD ** -0.5, k.rn[:, 0:3, :], ALU.mult, ALU.mult))
    v.tensor_tensor(k.sT[:, 3:6, :], k.sT[:, 3:6, :], k.rn[:, 3:6, :], ALU.mult).then_inc(k.qk_normed.sem, 1)
    slopes = alibi(DH)
    for m_ in range(NMAP):
        b = J.take(v, "dve", ("sc", m_), lay)
        v.scalar_tensor_tensor(k.prob[:, m_, :, :], k.dist[:, :, :], -slopes[m_ // 2], shaped(ps[b][:, :], TB, S),
                               ALU.mult, ALU.add).then_inc(J.read["dve"], 1)
        J.evac(v, ("sc", m_), lay)
        st.link(v.tensor_reduce(k.mx[:, m_, :], k.prob[:, m_, :, :], AX.X, ALU.max))
        v.tensor_scalar(k.mx[:, m_, :], k.mx[:, m_, :], -1.0, None, ALU.mult).then_inc(k.sc_max.sem, 1)
    wait(k.lam_exp)
    st.link(v.tensor_tensor(k.lam[:, 4:5], k.lam[:, 3:4], k.lam[:, 2:3], ALU.subtract))
    st.link(v.tensor_tensor(k.lam[:, 5:6], k.lam[:, 4:5], k.row[:, R_INIT:R_INIT + 1], ALU.subtract))
    for h in range(DH):
        wait(k.sc_exp, 2 * h + 2)
        st.link(v.reciprocal(k.ssum[:, 2 * h:2 * h + 2, :], k.ssum[:, 2 * h:2 * h + 2, :]))
        st.link(v.tensor_scalar(k.ssum[:, 2 * h + 1, :], k.ssum[:, 2 * h + 1, :], k.lam[:, 5:6], None, ALU.mult))
        for qb in range(TB):
            st.done(v.tensor_scalar(k.prob[:, 2 * h, qb, :], k.prob[:, 2 * h, qb, :], k.ssum[:, 2 * h, qb:qb + 1], None, ALU.mult))
        st.settle()
        for qb in range(TB):
            m = v.scalar_tensor_tensor(k.prob[:, 2 * h, qb, :], k.prob[:, 2 * h + 1, qb, :], k.ssum[:, 2 * h + 1, qb:qb + 1],
                                       k.prob[:, 2 * h, qb, :], ALU.mult, ALU.add)
            st.done(m) if qb == 0 else m.then_inc(k.attn_ready.sem, 1)
    wait(k.od_sq)
    v.tensor_reduce(k.onorm[:, :], shaped(k.od2.rearrange("p a b -> p (a b)"), 12, HD), AX.X, ALU.add).then_inc(k.od_ss.sem, 1)
    wait(k.od_rstd)
    od = k.od.rearrange("p a (h e) -> p (a h) e", e=HD)
    v.tensor_tensor(od, od, bc(k.onorm[:, :].unsqueeze(2), 12, HD), ALU.mult).then_inc(k.od_ready.sem, 1)
    J.evac(v, ("yd", 1), lay)
    for g, (dr, hp, tb) in enumerate(groups()):
        b = J.take(v, "dve", ("gr", g), lay)
        for p in range(PAIRS):
            col = dr * GH + 2 * p + hp
            m = v.scalar_tensor_tensor(k.E[:, 3 * g + p, :], ps[b][:, p * P:(p + 1) * P], k.gsum_c[:, tb, col:col + 1],
                                       c["pen_b" if dr else "pen_f"], ALU.subtract, ALU.max)
            st.done(m) if p < 2 else m.then_inc(J.read["dve"], 1)
    for hp in range(2):
        for tb in range(TB):
            b = J.take(v, "dve", ("kk", hp, tb), lay)
            gs = [groups().index((dr, hp, tb)) for dr in range(2)]
            wait(k.ES_ready, gs[1] + 1)
            for dr, g in enumerate(gs):
                for p in range(PAIRS):
                    col = dr * GH + 2 * p + hp
                    m = v.scalar_tensor_tensor(k.A[:, 3 * g + p, :], ps[b][:, p * P:(p + 1) * P], k.beta[:, tb, col:col + 1],
                                               k.ES[:, 3 * g + p, :], ALU.mult, ALU.mult)
                    st.done(m) if (dr, p) != (1, 2) else m.then_inc(J.read["dve"], 1)
            b = J.take(v, "dve", ("qk", hp, tb), lay)
            for dr, g in enumerate(gs):
                m = v.tensor_tensor(k.AQ[:, 3 * g:3 * g + 3, :], shaped(ps[b][:, 0:384], 3, P), k.E[:, 3 * g:3 * g + 3, :], ALU.mult)
                st.done(m) if dr == 0 else m.then_inc(J.read["dve"], 1)
    mask = lambda name, n=MATS: bc(c[name].unsqueeze(1), n, P)
    J.evac(v, ("at", GRP - 1), lay)
    J.evac(v, ("qt", GRP - 1), lay)
    st.done(v.tensor_tensor(k.DM[:, :, :], k.A[:, :, :], mask("bd8"), ALU.mult))
    v.tensor_tensor(k.DT[:, :, :], k.AT[:, :, :], mask("bd8"), ALU.mult).then_inc(k.D_ready.sem, 1)
    wait(k.D_ready)
    st.settle()
    st.done(v.tensor_tensor(k.T[:, :, :], mask("ident"), k.DM[:, :, :], ALU.subtract))
    v.tensor_tensor(k.TT[:, :, :], mask("ident"), k.DT[:, :, :], ALU.subtract).then_inc(k.P0_ready.sem, 1)
    wait(k.P0_ready)

    def accumulate(key, M, g, op):
        b = J.take(v, "dve", key, lay)
        v.tensor_tensor(M[:, 3 * g:3 * g + 3, :], M[:, 3 * g:3 * g + 3, :], shaped(ps[b][:, 0:384], 3, P), op)\
         .then_inc(J.read["dve"], 1)

    def blocks_below(lv, g):
        v.tensor_tensor(k.LT[:, 3 * g:3 * g + 3, :], k.AT[:, 3 * g:3 * g + 3, :], mask(("m8", "m16", "m32")[lv], 3),
                        ALU.mult).then_inc(k.LT_ready.sem, 1)

    for key, M in (("p1", k.T), ("p1t", k.TT)):
        for g in range(GRP):
            accumulate((key, g), M, g, ALU.add)
    J.evac(v, ("p1t", GRP - 1), lay)
    for g in range(GRP):
        accumulate(("t8", g), k.T, g, ALU.add)
    for g in range(GRP):
        accumulate(("t8t", g), k.TT, g, ALU.add)
        blocks_below(0, g)
    for lv in range(3):
        J.evac(v, ("t8t", GRP - 1) if lv == 0 else ("tyt", lv - 1, GRP - 1), lay)
        for g in range(GRP):
            if lv < 2:
                accumulate(("ty", lv, g), k.T, g, ALU.subtract)
            accumulate(("tyt", lv, g), k.TT, g, ALU.subtract)
            if lv < 2:
                blocks_below(lv + 1, g)
    wait(k.conv_done)
    for n in range(4):
        where = [(n // 2, n % 2), (1 - n // 2, 1 - n % 2)]
        b = J.take(v, "dve", ("v", n), lay)
        v.tensor_copy(k.v, ps[b][:, 0:384]).then_inc(J.read["dve"], 1)
        if n:
            J.evac(v, ("ao", n - 1), lay)
            b = J.take(v, "dve", ("qs", n), lay)
            for dr, (tb, par) in enumerate(where):
                rows = slice(par * 64, par * 64 + 64)
                m = v.tensor_tensor(shaped(k.qse[rows, :], GH, HD), shaped(ps[b][rows, 0:384], GH, HD),
                                    k.eg[rows, tb, dr * GH:(dr + 1) * GH].unsqueeze(2).to_broadcast([64, GH, HD]), ALU.mult)
                st.done(m) if dr == 0 else m.then_inc(J.read["dve"], 1)
        if n < 3:
            for dr, (tb, par) in enumerate(where):
                b = J.take(v, "dve", ("kv", n, dr), lay)
                for p in range(PAIRS):
                    for hp in range(2):
                        rows = slice(hp * 64, hp * 64 + 64)
                        s_ = k.st[rows, dr, p, hp * 64:hp * 64 + 64]
                        ch = tb * 2 + par
                        m = v.scalar_tensor_tensor(s_, s_, k.gl[rows, ch, dr * 3 + p:dr * 3 + p + 1],
                                                   ps[b][rows, p * P + hp * 64:p * P + hp * 64 + 64], ALU.mult, ALU.add)
                        st.done(m) if (p, hp) != (2, 1) else m.then_inc(J.read["dve"], 1)
        if n:
            st.settle()
            J.evac(v, ("qs", n), lay)
        if n >= 2:
            for dr, (tb, par) in enumerate(where):
                rows = slice(par * 64, par * 64 + 64)
                st.done(v.tensor_tensor(k.qse[rows, :], k.qse[rows, :], k.o[rows, tb, :], ALU.add))
            st.settle()
        b = J.take(v, "dve", ("ao", n), lay)
        for dr, (tb, par) in enumerate(where):
            rows = slice(par * 64, par * 64 + 64)
            if n == 0:
                m = v.tensor_copy(k.o[rows, tb, :], ps[b][rows, 0:384])
            else:
                m = v.tensor_tensor(k.o[rows, tb, :], k.qse[rows, :], ps[b][rows, 0:384], ALU.add)
            st.done(m) if dr == 0 else m.then_inc(J.read["dve"], 1)
    b = J.take(v, "dve", "cm", lay)
    for i in range(2):
        m = v.scalar_tensor_tensor(k.cxc[:, i, :], ps[b][:, 0:S], -1.0 / CONV_CH, k.cacc[:, i, :], ALU.mult, ALU.add)
        st.done(m) if i == 0 else m.then_inc(J.read["dve"], 1)
    wait(k.o_sq)
    v.tensor_reduce(k.onorm[:, :], shaped(k.o2.rearrange("p a b -> p (a b)"), 12, HD), AX.X, ALU.add).then_inc(k.o_ss.sem, 1)
    J.evac(v, "cv", lay)
    st.link(v.reciprocal(k.crs, k.crs))
    st.link(v.tensor_tensor(k.cxc[:, :, :], k.cxc[:, :, :], bc(k.crs.unsqueeze(1), 2, S), ALU.mult))
    for i in range(2):
        m = v.tensor_scalar(k.cxc[:, i, :], k.cxc[:, i, :], k.vec[:, V_LNW + i:V_LNW + i + 1], k.vec[:, V_LNB + i:V_LNB + i + 1],
                            ALU.mult, ALU.add)
        st.done(m) if i == 0 else m.then_inc(k.conv_lin.sem, 1)
    wait(k.o_rstd)
    o = k.o.rearrange("p a (h e) -> p (a h) e", e=HD)
    st.link(v.tensor_tensor(o, o, bc(k.onorm[:, :].unsqueeze(2), 12, HD), ALU.mult))
    v.tensor_tensor(k.o[:, :, :], k.o[:, :, :], k.zs[:, :, :], ALU.mult).then_inc(k.o_ready.sem, 1)
    dve_post(k, v, st, lay, 0, k.x_mixed)
    wait(k.h_rstd, 2)
    for tb in range(TB):
        v.tensor_scalar(k.xn[:, tb, :], k.x[:, tb, :], k.stat[:, 8 + tb:9 + tb], None, ALU.mult).then_inc(k.h_scaled.sem, 1)
    dve_evac_h(k, v, J, "h2", V_MLP, lay)
    J.evac(v, ("h2", 2), lay)
    J.evac(v, ("h2", 3), lay)
    dve_experts(k, v, "ff", FF_SLOTS, k.FF, lay, lambda i, u: k.FF.r[u % 2])
    dve_post(k, v, st, lay, 1, k.x_done)
    wait(k.x_done)
    st.close("vector")


def act_squares_x(k, a, sa, lay, n0):
    for tb in range(TB):
        a.activation(k.junk, k.x[:, tb, :], ACT.Square, accum_out=k.stat[:, tb:tb + 1]).then_inc(k.h_squares.sem, 1)
        a.wait_ge(k.h_squares.sem, k.h_squares.at(n0 + tb + 1, lay))


def act_evac_h(k, a, J, key, col, lay):
    for i in (0, 2):
        b = J.take(a, "act", (key, i), lay)
        for kk in range(2):
            kt = 2 * i + kk
            m = a.activation(k.hT[:, kt, :], k.psum[b][:, kk * S:(kk + 1) * S], ACT.Copy, scale=k.vec[:, col + kt:col + kt + 1])
        m.then_inc(J.read["act"], 1)


def act_y_squares(k, a, lay, n0):
    for i in range(4):
        a.activation(k.junk[:, 0:512], k.psum[4 + i][:, :], ACT.Square, accum_out=k.stat[:, 2 + i:3 + i]).then_inc(k.y_squares.sem, 1)
        a.wait_ge(k.y_squares.sem, k.y_squares.at(n0 + i + 1, lay))


def act_layer(k, a, lay):
    J, ps = k.J1, k.psum
    sa = Steps(a, k.act_step, ACT_STEPS, lay)
    wait = lambda sig, n=None: a.wait_ge(sig.sem, sig.at(n, lay))
    a.dma_start(k.vec[:, :], k.dram["vec1"][bass.ds(lay, 1)].rearrange("a p n -> (a p) n")).then_inc(k.params_loaded, 16)
    a.dma_start(k.row[:, :], k.dram["row1"][bass.ds(lay, 1), :].to_broadcast([P, RCOLS])).then_inc(k.params_loaded, 16)
    act_squares_x(k, a, sa, lay, 0)
    a.wait_ge(k.params_loaded, lay * 32 + 32)
    act_evac_h(k, a, J, "h", V_PRE, lay)

    def copy(key, dst, n, func=ACT.Copy, **kw):
        b = J.take(a, "act", key, lay)
        a.activation(dst, n(ps[b]) if callable(n) else ps[b][:, 0:n], func, **kw).then_inc(J.read["act"], 1)

    for tb in range(TB):
        b = J.take(a, "act", ("zb", tb), lay)
        sa.done(a.activation(k.zs[:, tb, :], ps[b][:, 0:384], ACT.Silu))
        a.activation(k.ba[:, tb, :], ps[b][:, 384:408], ACT.Copy).then_inc(J.read["act"], 1)
    for tb in range(TB):
        copy(("dv", tb), k.dv[:, tb, :], 384)
    for i in range(5):
        n = 1 if i == 4 else 2
        copy(("s", i), k.raw[:, 2 * i:2 * i + n, 1:S + 1], lambda t, n=n: shaped(t[:, 0:n * S], n, S))
    copy("cg", k.csig[:, :, :], lambda t: shaped(t[:, :], 2, S), ACT.Sigmoid)
    for i in range(3):
        b = J.take(a, "act", ("d", i), lay)
        for kk in range(2):
            t = 2 * i + kk
            m = a.activation(k.qkd[:, t, :], ps[b][:, kk * S:(kk + 1) * S], ACT.Copy, scale=DD ** -0.5 if t < 3 else 1.0)
            sa.done(m) if kk == 0 else m.then_inc(J.read["act"], 1)
    wait(k.gate_arg)
    sa.link(a.activation(k.ge[:, :, :], k.gb[:, :, :], ACT.Exp))
    sa.done(a.activation(k.ge[:, :, :], k.ge[:, :, :], ACT.Ln, bias=1.0))
    J.evac(a, ("zb", 1), lay)
    sa.done(a.activation(k.beta[:, :, :], k.ba[:, :, 0:12], ACT.Exp, scale=-1.0))
    a.activation(k.negA[:, :], k.row[:, R_ALOG:R_ALOG + 12], ACT.Exp).then_inc(k.gate_exp.sem, 1)
    wait(k.lam_arg)
    a.activation(k.lam[:, 2:4], k.lam[:, 0:2], ACT.Exp).then_inc(k.lam_exp.sem, 1)
    b = J.take(a, "act", "gl", lay)
    a.activation(k.gl[:, :, :], shaped(ps[b][:, 0:24], 4, 6), ACT.Exp).then_inc(J.read["act"], 1)
    wait(k.gc_ready)
    sa.done(a.activation(k.eg[:, :, :], k.gsum_c[:, :, 0:12], ACT.Exp))
    a.activation(k.ekd[:, :, :], k.ekd[:, :, :], ACT.Exp).then_inc(k.gc_exp.sem, 1)
    wait(k.sconv)
    sa.link(a.activation(k.sT[:, :, :], k.sT[:, :, :], ACT.Silu))
    a.activation(k.sq[:, :, :], k.sT[:, 0:6, :], ACT.Square).then_inc(k.sq_ready.sem, 1)
    for i in range(3):
        copy(("l2", i), k.rn[:, 2 * i:2 * i + 2, :], lambda t: shaped(t[:, :], 2, S), ACT.Sqrt, bias=k.eps6)
    for m_ in range(NMAP):
        wait(k.sc_max, m_ + 1)
        for qb in range(TB):
            m = a.activation(k.prob[:, m_, qb, :], k.prob[:, m_, qb, :], ACT.Exp, bias=k.mx[:, m_, qb:qb + 1],
                             accum_out=k.ssum[:, m_, qb:qb + 1])
            m.then_inc(k.sc_exp2.sem if qb == 0 else k.sc_exp.sem, 1)

    def out_head(h):
        copy(("av", h), k.od[:, :, h * HD:(h + 1) * HD], lambda t: shaped(t[:, 0:2 * HD], 2, HD))

    for h in range(DH):
        copy(("ar", h), k.ATd[h % 2][:, :, :], lambda t: shaped(t[:, :], TB, S))
        if h:
            out_head(h - 1)
    out_head(DH - 1)
    wait(k.sub_ready)
    for i in range(2):
        n = 2 if i == 0 else 1
        copy(("yd", i), k.hT[:, 2 + 2 * i:2 + 2 * i + n, :], lambda t, n=n: shaped(t[:, 0:n * S], n, S), scale=k.sub[:, :])
    for g in range(GRP):
        J.evac(a, ("gr", g), lay)
        E = k.E[:, 3 * g:3 * g + 3, :]
        a.activation(E, E, ACT.Exp, scale=-1.0).then_inc(k.E_exp.sem, 1)
    for name, dst in (("kn", k.Kn), ("vn", k.Vn)):
        for tb in range(TB):
            copy((name, tb), dst[:, tb, :], 384)

    def stack(key, M, g):
        copy(key, M[:, 3 * g:3 * g + 3, :], lambda t: shaped(t[:, 0:384], 3, P))

    for g in range(GRP):
        stack(("at", g), k.AT, g)
        stack(("qt", g), k.AQT, g)
    for key, M in (("d2", k.D2), ("d2t", k.D2T)):
        for g in range(GRP):
            stack((key, g), M, g)
    for key, M in (("d4", k.D4), ("d4t", k.D4T)):
        for g in range(GRP):
            stack((key, g), M, g)
    J.evac(a, ("t8t", GRP - 1), lay)
    for i in range(2):
        a.dma_start(k.post[i], k.dram["post1"][bass.ds(lay, 1), i * D:(i + 1) * D].to_broadcast([P, D])).then_inc(k.post_loaded, 16)
    for lv in range(3):
        for g in range(GRP):
            stack(("y", lv, g), k.Y, g)
    for dr in range(2):
        for tb in range(TB):
            copy(("w", dr, tb), k.nwT[:, dr, tb, :, :], lambda t: shaped(t[:, 0:384], 3, P), scale=-1.0)
    J.evac(a, "cm", lay)
    a.activation(k.csq[:, :, :], k.cxc[:, :, :], ACT.Square).then_inc(k.csq_ready.sem, 1)
    copy("cv", k.crs, S, ACT.Sqrt, scale=1.0 / CONV_CH, bias=k.eps5)
    wait(k.conv_lin)
    a.activation(k.hT[:, 0:2, :], k.cxc[:, :, :], ACT.Silu).then_inc(k.conv_out.sem, 1)
    for i in range(2):
        n = 2 if i == 0 else 1
        copy(("yx", i), k.hT[:, 5 + 2 * i:5 + 2 * i + n, :], lambda t, n=n: shaped(t[:, 0:n * S], n, S), scale=k.vec[:, V_DN:V_DN + 1])
    wait(k.y_acc)
    act_y_squares(k, a, lay, 0)
    wait(k.x_mixed)
    act_squares_x(k, a, sa, lay, 2)
    act_evac_h(k, a, J, "h2", V_MLP, lay)
    act_experts(k, a, FF_SLOTS, k.FF, lay, ACT.Relu)
    wait(k.y_ff)
    act_y_squares(k, a, lay, 4)
    wait(k.x_done)
    sa.close("scalar")


def act_experts(k, a, n, X, lay, func):
    base = X.base(lay)
    with a.Fori(0, n // 4) as i:
        for u in range(4):
            a.wait_ge(X.up, base + i * 4 + (u + 1))
            a.activation(X.r[u % 2], k.psum[u][:, 0:S], func).then_inc(X.acted, 1)


def pool_rsqrt(k, p, sp, v, scale, eps, sig):
    n = list(v.shape)
    sp.link(p.tensor_tensor(v, v, scale.to_broadcast(n), ALU.mult))
    sp.link(p.tensor_tensor(v, v, eps.to_broadcast(n), ALU.add))
    p.tensor_tensor(v, v, k.minus_half.to_broadcast(n), ALU.pow).then_inc(sig.sem, 1)


def pool_layer(k, p, lay):
    J, c = k.J1, k.c
    sp = Steps(p, k.pool_step, POOL_STEPS, lay)
    wait = lambda sig, n=None: p.wait_ge(sig.sem, sig.at(n, lay))

    def x_rstd(n):
        wait(k.h_squares, 2 * n)
        sp.link(p.tensor_tensor(k.stat[:, 8:10], k.stat[:, 0:2], k.inv_d.to_broadcast([P, 2]), ALU.mult))
        sp.link(p.tensor_tensor(k.stat[:, 8:10], k.stat[:, 8:10], k.eps6.to_broadcast([P, 2]), ALU.add))
        p.tensor_tensor(k.stat[:, 8:10], k.stat[:, 8:10], k.minus_half.to_broadcast([P, 2]), ALU.pow).then_inc(k.h_rstd.sem, 1)

    def y_rstd(n):
        wait(k.y_squares, 4 * n)
        sp.link(p.tensor_tensor(k.stat[:, 8:10], k.stat[:, 2:6:2], k.stat[:, 3:6:2], ALU.add))
        pool_rsqrt(k, p, sp, k.stat[:, 8:10], k.inv_d, k.eps6, k.y_rstd)

    x_rstd(1)
    J.evac(p, ("av", DH - 1), lay)
    p.tensor_tensor(k.od2[:, :, :], k.od[:, :, :], k.od[:, :, :], ALU.mult).then_inc(k.od_sq.sem, 1)
    wait(k.od_ss)
    pool_rsqrt(k, p, sp, k.onorm[:, :], k.inv_hd, k.eps5, k.od_rstd)
    for g in range(GRP):
        wait(k.E_exp, g + 1)
        p.tensor_tensor(k.ES[:, 3 * g:3 * g + 3, :], k.E[:, 3 * g:3 * g + 3, :], bc(c["notdiag"].unsqueeze(1), 3, P), ALU.mult)\
         .then_inc(k.ES_ready.sem, 1)
    wait(k.beg_ready)
    J.evac(p, ("vn", 1), lay)
    for dr in range(2):
        for tb in range(TB):
            for src, dst, f in ((k.Kn, k.kbg, k.beg), (k.Kn, k.kdec, k.ekd), (k.Vn, k.vb, k.beta)):
                m = p.tensor_tensor(shaped(dst[:, dr, tb, :], GH, HD), shaped(src[:, tb, :], GH, HD),
                                    bc(f[:, tb, dr * GH:(dr + 1) * GH].unsqueeze(2), GH, HD), ALU.mult)
                if (dr, tb) == (1, 1) and dst is k.vb:
                    m.then_inc(k.kv_scaled.sem, 1)
                else:
                    sp.done(m)
    J.evac(p, "ca", lay)
    for tap in range(CONV_W):
        w = bc(k.vec[:, V_TAP + tap:V_TAP + CONV_W + tap + 1:CONV_W].unsqueeze(2), 2, S)
        sp.link(p.tensor_tensor(k.ctap[:, :, :], k.cpad[:, :, tap:tap + S], w, ALU.mult))
        add = k.ctap[:, :, :] if tap else bc(k.vec[:, V_CB:V_CB + 2].unsqueeze(2), 2, S)
        if tap == 0:
            m = p.tensor_tensor(k.cacc[:, :, :], k.ctap[:, :, :], add, ALU.add)
        else:
            m = p.tensor_tensor(k.cacc[:, :, :], k.cacc[:, :, :], add, ALU.add)
        if tap == CONV_W - 1:
            m.then_inc(k.conv_done.sem, 1)
        else:
            sp.link(m)
    J.evac(p, ("ao", 3), lay)
    p.tensor_tensor(k.o2[:, :, :], k.o[:, :, :], k.o[:, :, :], ALU.mult).then_inc(k.o_sq.sem, 1)
    wait(k.o_ss)
    pool_rsqrt(k, p, sp, k.onorm[:, :], k.inv_hd, k.eps6, k.o_rstd)
    y_rstd(1)
    x_rstd(2)
    y_rstd(2)
    wait(k.x_done)
    sp.close("gpsimd")


def sp_layers(k, sp):
    w = k.dram["w1"]

    def load(r, g):
        sp.dma_start(k.ring[r], w[bass.ds(g, 1)].rearrange("a p n -> (a p) n")).then_inc(k.weights_loaded[r], 16)

    def used(pos, lay, seg="mix"):
        sp.wait_ge(k.weights_used, STREAM.used(seg, pos, lay))

    for pos in range(RING):
        load(pos, pos)
    with sp.Fori(0, DEPTH) as lay:
        base = lay * LAYER_SLOTS
        for pos in range(RING, MIX_SLOTS):
            used(pos - RING, lay)
            load(pos % RING, base + pos)
        for j in range(RING):
            used(STREAM.prior[("ff", 0, j)], lay)
            load(j, base + (MIX_SLOTS + j))
        with sp.Fori(0, FF_SLOTS // 4 - 1) as i:
            for u in range(4):
                sp.wait_ge(k.weights_used, STREAM.used("ff", u, lay) + i * 4)
                load(u, base + i * 4 + (MIX_SLOTS + 4 + u))
        for j in range(RING):
            used(FF_SLOTS - RING + j, lay, "ff")
            load(j, base + (LAYER_SLOTS + j))


N_MOD = 6
Y_C, Y_BMOD, Y_QN, Y_KVN, Y_PS = 0, 16, 112, 115, 117
YCOLS = Y_PS + 8
SH1, SC1, G1, SH2, SC2, G2 = (8 * i for i in range(N_MOD))
TOK = S + CTX
SCALE = (NOPE + ROPE) ** -0.5
W_GROUPS = S // 4


def both(i):
    return "act" if i % 2 == 0 else "dve"


def mla_jobs():
    j = [("mod", "dve")]
    j += [(("xt", i), both(i)) for i in range(4)] + [(("ct", i), both(i)) for i in range(4)]
    j += [(("zq", i), "act") for i in range(3)] + [(("zk", i), "act") for i in range(2)] + [("zr", "act")]
    j += [("sq", "act"), ("sk", "act"), ("rk", "dve")]
    j += [(("uq", i), "act") for i in range(6)]
    j += [(("rq", i), "dve") for i in range(2)]
    j += [(("uk", i), both(i)) for i in range(MH)]
    j += [(("uv", i), both(i)) for i in range(8)]
    j += [(("s", 0), "act"), (("s", 1), "act")]
    for n in range(2 * MH):
        j += [(("pt", n), "act")] + [(("s", n + 2), "act")] * (n + 2 < 2 * MH)
        j += [(("o", n // 2), "dve")] * (n % 2)
    j += [(("g", i), "act") for i in range(2)]
    return j


def peer_jobs():
    j = [(("xt", i), both(i)) for i in range(4)]
    j += [(("q", i), both(i)) for i in range(8)]
    j += [(("s", i), "act") for i in range(8)]
    j += [(("rt", i), "act") for i in range(2)]
    j += [(("g", i), "act") for i in range(2)]
    return j


def pool_jobs():
    j = [(("xt", i), both(i)) for i in range(4)]
    j += [(("z", i), "act") for i in range(4)]
    j += [(("gp", i), both(i)) for i in range(4)]
    j += [(("g", i), "act") for i in range(2)]
    return j


def plan_memory2(k):
    b = Arena(k.sb, k.free)
    k.hot = [shaped(b.take(1024), 2, 4, P)]
    k.rT = b.take(3, S)
    b.take(SPLIT - (b.off - k.late))
    k.vec2 = b.take(YCOLS)
    k.mod = b.take(2, 48)
    k.bn = b.take(TB, 2, 6)
    k.mv = b.take(TB, 2)
    k.exp_at = b.off
    hot = b.take(1024)
    k.hot.append(shaped(hot, 2, 4, P))
    work = b.off
    k.W = b.take(S, P)
    m = Arena(k.sb, work)
    end = work + S * P
    k.mod_row = k.sb[0:2, end - DEPTH * N_MOD * D:end]
    k.cmod = m.take(16)
    k.cs = m.take(KT, 2)
    k.hc = m.take(KT, TOK)
    k.ctx = m.take(TB, D)
    k.zq, k.zkv, k.kr = m.take(3, S), m.take(2, TOK), m.take(TOK)
    k.zsq, k.zksq = m.take(3, S), m.take(2, TOK)
    k.rq, k.rkv = m.take(S), m.take(TOK)
    k.qn, k.qr, k.qrot = m.take(MH, S), m.take(4, S), m.take(4, S)
    k.kn, k.vv = m.take(MH, TOK), m.take(4, D)
    k.krot = m.take(S)
    k.p = [m.take(TOK) for _ in range(2)]
    k.pT = [m.take(4, S) for _ in range(2)]
    k.amx, k.asum = m.take(16), m.take(16)
    k.oT = k.hT
    n = Arena(k.sb, m.off)
    k.gbc, k.lng, k.lnb, k.diag = n.take(D), n.take(D), n.take(D), n.take(8, P)
    k.ptmp = [k.diag.rearrange("p a b -> p (a b)")[:, i * 512:(i + 1) * 512] for i in range(2)]
    r = Arena(k.sb, work)
    k.qT = r.take(HH, S)
    k.s = r.take(TB, HH, NK)
    k.s2 = r.take(HH, NK)
    k.val, k.ixf = r.take(HH, TOPK), r.take(HH, TOPK)
    k.ix = r.take(HH, TOPK).bitcast(U32)
    k.cand, k.cand2, k.eq = (r.take(PH, TOPK * TOPK) for _ in range(3))
    k.top, k.posf, k.posa, k.posb = (r.take(PH, TOPK) for _ in range(4))
    k.pos, k.pa_, k.pb_ = (r.take(PH, TOPK).bitcast(U32) for _ in range(3))
    k.gsum = r.take(PH)
    k.sel = r.take(TB, 3, PH, TOPK)
    q = Arena(k.sb, work)
    LZ = S + 24
    k.zp = q.take(KT, LZ)
    k.za = [q.take(2, LZ) for _ in range(2)]
    k.pooled = q.take(KT, S)
    k.LZ = LZ
    k.inv_count = q.take(len(WINDOWS), S)


def pe_transpose(k, pe, J, key, src, it=None):
    for i in range(4):
        b = J.give(pe, (key, i), it)
        for kk in range(2):
            for tb in range(TB):
                t = pe.transpose(k.psum[b][:, kk * S + tb * P:kk * S + (tb + 1) * P],
                                 src[:, tb, (2 * i + kk) * P:(2 * i + kk + 1) * P], k.c["ident"])
        t.then_inc(J.filled, 1)


def pe_row(k, pe, J, sig, it=None):
    pe.wait_ge(k.diag_ready.sem, sig)
    for i in range(2):
        b = J.give(pe, (("g", i)), it)
        pe.matmul(k.psum[b][:, :], k.c["ones"], k.diag[:, 4 * i:4 * i + 4, :], start=True, stop=True).then_inc(J.filled, 1)


def pe_out(k, pe, seg, pos0, src):
    for s in range(4):
        w = slot(k, pe, seg, pos0 + s)
        for kk in range(2):
            kt = 2 * s + kk
            for tb in range(TB):
                for half in range(2):
                    m = pe.matmul(k.psum[4 + 2 * tb + half][:, :], src[:, kt, tb * P:(tb + 1) * P],
                                  w[:, kk * D + half * 512:kk * D + (half + 1) * 512], start=kt == 0, stop=kt == KT - 1)
        m.then_inc(k.weights_used, 1)
    pe.matmul(k.psum[0][:, 0:64], k.zero[:, :], k.zero_row[:, 0:64], start=True, stop=True).then_inc(k.y2_acc.sem, 1)


def pe_mla(k, pe):
    J, c, ps = k.J2, k.c, k.psum
    pe.wait_ge(k.c_ready, 1)
    def chunk(i, u, first):
        if not first:
            pe.wait_ge(k.mod_read, i * 2 + (u - 1))
        for h in range(2):
            pe.wait_ge(k.weights_loaded[2 * u + h], i * 16 + STREAM.loaded("mod", 2 * u + h))
            for q in range(4):
                m = pe.matmul(ps[4 + u][0:2, :], k.cs[:, 4 * h + q, :], k.ring[2 * u + h][:, q * 512:(q + 1) * 512],
                              start=(h, q) == (0, 0), stop=(h, q) == (1, 3))
            m.then_inc(k.weights_used, 1)

    for u in range(2):
        chunk(0, u, True)
    with pe.Fori(1, MOD_SLOTS // 4) as i:
        for u in range(2):
            chunk(i, u, False)
    pe.wait_ge(k.mod_read, MOD_SLOTS // 2)
    b = J.give(pe, "mod")
    for t in range(DEPTH * N_MOD * KT):
        pe.transpose(ps[b][:, 2 * t:2 * t + 2], k.mod_row[:, t * P:(t + 1) * P], c["ident"][0:2, 0:2])
    pe.matmul(ps[b][:, 256:320], k.zero[:, :], k.zero_row[:, 0:64], start=True, stop=True).then_inc(J.filled, 1)
    pe_transpose(k, pe, J, "xt", k.x)
    pe.wait_ge(k.mla_loaded, 32)
    pe_transpose(k, pe, J, "ct", k.ctx)
    J.evac(pe, ("ct", 2))
    J.evac(pe, ("ct", 3))
    rel = Release(k)
    for t, key in enumerate([("zq", 0), ("zq", 1), ("zq", 2), ("zk", 0), ("zk", 1), "zr"]):
        w = slot(k, pe, "mla", t // 2)
        n = S if t < 3 else TOK
        b = J.give(pe, key)
        for kt in range(KT):
            m = pe.matmul(ps[b][:, 0:n], w[:, (t % 2) * D + kt * P:(t % 2) * D + (kt + 1) * P], k.hc[:, kt, 0:n],
                          start=kt == 0, stop=kt == KT - 1)
            if kt == 0:
                rel.pay(m)
        m.then_inc(J.filled, 1)
        if t % 2:
            rel.owe()
    pe.wait_ge(k.z_squares, 1)
    b = J.give(pe, "sq")
    for i in range(3):
        m = pe.matmul(ps[b][:, 0:S], c["ones"], k.zsq[:, i, :], start=i == 0, stop=i == 2)
        rel.pay(m) if i == 0 else None
    m.then_inc(J.filled, 1)
    pe.wait_ge(k.z_squares, 2)
    b = J.give(pe, "sk")
    for i in range(2):
        m = pe.matmul(ps[b][:, :], c["ones"], k.zksq[:, i, :], start=i == 0, stop=i == 1)
    m.then_inc(J.filled, 1)
    J.evac(pe, "zr")
    b = J.give(pe, "rk")
    pe.matmul(ps[b][:, 0:S], c["rot"], k.kr[:, 0:S], start=True, stop=True).then_inc(J.filled, 1)
    pe.wait_ge(k.cq_ready, 1)
    for i in range(6):
        b = J.give(pe, ("uq", i))
        for kk in range(2):
            t = 2 * i + kk
            w = slot(k, pe, "mla", 3 + t // 5)
            if t % 5 == 0 and t:
                rel.owe()
            for kt in range(3):
                m = pe.matmul(ps[b][:, kk * S:(kk + 1) * S], w[:, (t % 5) * 384 + kt * P:(t % 5) * 384 + (kt + 1) * P],
                              k.zq[:, kt, :], start=kt == 0, stop=kt == 2)
                if kt == 0:
                    rel.pay(m)
        m.then_inc(J.filled, 1)
    rel.owe()
    J.evac(pe, ("uq", 5))
    for i in range(2):
        b = J.give(pe, ("rq", i))
        for kk in range(2):
            m = pe.matmul(ps[b][:, kk * S:(kk + 1) * S], c["rot"], k.qr[:, 2 * i + kk, :], start=True, stop=True)
            rel.pay(m)
        m.then_inc(J.filled, 1)
    pe.wait_ge(k.ckv_ready, 1)
    w = slot(k, pe, "mla", 6)
    for h in range(MH):
        b = J.give(pe, ("uk", h))
        for kt in range(2):
            m = pe.matmul(ps[b][:, :], w[:, h * 256 + kt * P:h * 256 + (kt + 1) * P], k.zkv[:, kt, :], start=kt == 0, stop=kt == 1)
        m.then_inc(J.filled, 1)
    rel.owe()
    w = slot(k, pe, "mla", 7)
    for i in range(8):
        tok, half = i // 2, i % 2
        b = J.give(pe, ("uv", i))
        for kt in range(2):
            m = pe.matmul(ps[b][:, :], k.zkv[:, kt, tok * P:(tok + 1) * P], w[:, kt * D + half * 512:kt * D + (half + 1) * 512],
                          start=kt == 0, stop=kt == 1)
            rel.pay(m) if kt == 0 else None
        m.then_inc(J.filled, 1)
    rel.owe()
    J.evac(pe, ("uk", 6))
    J.evac(pe, ("uk", 7))
    pe.wait_ge(k.rope_ready, 2)

    def score(n):
        h, qb = n // 2, n % 2
        r = (h % 2) * ROPE
        b = J.give(pe, ("s", n))
        m = pe.matmul(ps[b][:, :], k.qn[:, h, qb * P:(qb + 1) * P], k.kn[:, h, :], start=True, stop=False)
        rel.pay(m)
        pe.matmul(ps[b][:, :], k.qr[r:r + ROPE, h // 2, qb * P:(qb + 1) * P], k.kr[r:r + ROPE, :], start=False, stop=True)\
          .then_inc(J.filled, 1)

    score(0)
    score(1)
    J.evac(pe, ("uv", 6))
    J.evac(pe, ("uv", 7))
    for n in range(2 * MH):
        h, qb = n // 2, n % 2
        pe.wait_ge(k.p_ready, n + 1)
        b = J.give(pe, ("pt", n))
        for kb in range(4):
            m = pe.transpose(ps[b][:, kb * P:(kb + 1) * P], k.p[n % 2][:, kb * P:(kb + 1) * P], c["ident"])
        m.then_inc(J.filled, 1)
        if n + 2 < 2 * MH:
            score(n + 2)
        if qb:
            J.evac(pe, ("pt", n))
            b = J.give(pe, ("o", h))
            for kb in range(4):
                m = pe.matmul(ps[b][:, 0:S], k.vv[:, kb, h * VD:(h + 1) * VD], k.pT[h % 2][:, kb, :], start=kb == 0, stop=kb == 3)
            m.then_inc(J.filled, 1)
    J.evac(pe, ("o", MH - 1))
    pe_row(k, pe, J, 1)
    J.evac(pe, ("g", 1))
    pe_out(k, pe, "mla", 8, k.oT)


def pe_peer(k, pe, l):
    J, c, ps = k.J3, k.c, k.psum
    pe.wait_ge(k.x2_done.sem, 2 * l + 1)
    pe_transpose(k, pe, J, "xt", k.x, l)
    J.evac(pe, ("xt", 2), l)
    J.evac(pe, ("xt", 3), l)
    seg = f"qk{l}"
    rel = Release(k)
    for i in range(8):
        w = slot(k, pe, seg, i)
        b = J.give(pe, ("q", i), l)
        for kk in range(2):
            for kt in range(KT):
                m = pe.matmul(ps[b][:, kk * S:(kk + 1) * S], w[:, kk * D + kt * P:kk * D + (kt + 1) * P], k.hT[:, kt, :],
                              start=kt == 0, stop=kt == KT - 1)
                rel.pay(m) if kt == 0 else None
        m.then_inc(J.filled, 1)
        rel.owe()
    w = slot(k, pe, seg, 8)
    J.evac(pe, ("q", 6), l)
    J.evac(pe, ("q", 7), l)
    for i in range(8):
        tb, part = i // 4, i % 4
        b = J.give(pe, ("s", i), l)
        for a in range(4):
            hh = 4 * part + a
            m = pe.matmul(ps[b][:, a * P:(a + 1) * P], k.qT[:, hh, tb * P:(tb + 1) * P], w[:, hh * P:(hh + 1) * P], start=True, stop=True)
            rel.pay(m)
        m.then_inc(J.filled, 1)
    rel.owe()
    for i, (arr, n) in enumerate(((0, 2), (2, 1))):
        if i == 0:
            pe.wait_ge(k.sel_ready.sem, k.sel_ready.at(2, l))
        b = J.give(pe, ("rt", i), l)
        for a in range(n):
            for tb in range(TB):
                m = pe.transpose(ps[b][:, a * S + tb * P:a * S + (tb + 1) * P],
                                 k.sel[:, tb, arr + a, :, :].rearrange("p h k -> p (h k)"), c["ident"])
                rel.pay(m)
        m.then_inc(J.filled, 1)
    J.evac(pe, ("rt", 1), l)
    base = l * W_GROUPS

    def group(i, u, first):
        pe.wait_ge(k.hot_ready, i * 4 + (base + u + 1))
        if not first:
            pe.wait_ge(k.w_read, i * 4 + (base + u - 3))
        for t in range(4):
            m = pe.matmul(ps[u][:, t * P:(t + 1) * P], k.hot[u % 2][:, 0, t, :], k.hot[u % 2][:, 1, t, :], start=True, stop=True)
        m.then_inc(k.w_filled, 1)

    for u in range(4):
        group(0, u, True)
    with pe.Fori(1, W_GROUPS // 4) as i:
        for u in range(4):
            group(i, u, False)
    pe.wait_ge(k.w_read, base + W_GROUPS)
    pe_experts(k, pe, EXP_SLOTS, k.PX, l, k.y_exp)
    pe_row(k, pe, J, 2 * l + 2, l)


def pe_pool(k, pe):
    J, ps = k.J4, k.psum
    pe.wait_ge(k.x2_done.sem, 2)
    pe_transpose(k, pe, J, "xt", k.x)
    J.evac(pe, ("xt", 2))
    J.evac(pe, ("xt", 3))
    rel = Release(k)
    for i in range(4):
        w = slot(k, pe, "pool", i)
        b = J.give(pe, ("z", i))
        for kk in range(2):
            for kt in range(KT):
                m = pe.matmul(ps[b][:, kk * S:(kk + 1) * S], w[:, kk * D + kt * P:kk * D + (kt + 1) * P], k.hT[:, kt, :],
                              start=kt == 0, stop=kt == KT - 1)
                rel.pay(m) if kt == 0 else None
        m.then_inc(J.filled, 1)
        rel.owe()
    w = slot(k, pe, "pool", 4)
    for g in range(4):
        pe.wait_ge(k.pooled_ready, g + 1)
        b = J.give(pe, ("gp", g))
        for dt in range(2):
            for kt in range(2):
                o = (g * 4 + dt * 2 + kt) * P
                m = pe.matmul(ps[b][:, dt * S:(dt + 1) * S], w[:, o:o + P], k.pooled[:, 2 * g + kt, :], start=kt == 0, stop=kt == 1)
                rel.pay(m)
        m.then_inc(J.filled, 1)
    rel.owe()
    pe.wait_ge(k.diag_ready.sem, 3)
    J.evac(pe, ("gp", 2))
    J.evac(pe, ("gp", 3))
    for i in range(2):
        b = J.give(pe, ("g", i))
        m = pe.matmul(ps[b][:, 0:64], k.zero[:, :], k.zero_row[:, 0:64], start=True, stop=True)
        rel.pay(m)
        pe.matmul(ps[b][:, :], k.c["ones"], k.diag[:, 4 * i:4 * i + 4, :], start=True, stop=True).then_inc(J.filled, 1)
    J.evac(pe, ("g", 1))
    pe_out(k, pe, "pool", 5, k.hT)


def mod_evac(k, eng, J, who, key, dst, shift, scale, it=None):
    for i in range(4):
        if J.who[J.at[(key, i)]] != who:
            continue
        b = J.take(eng, who, (key, i), it)
        for kk in range(2):
            kt = 2 * i + kk
            src = k.psum[b][:, kk * S:(kk + 1) * S]
            if who == "dve":
                m = eng.tensor_scalar(dst(kt), src, scale[:, kt:kt + 1], shift[:, kt:kt + 1], ALU.mult, ALU.add)
            else:
                m = eng.activation(dst(kt), src, ACT.Identity, scale=scale[:, kt:kt + 1], bias=shift[:, kt:kt + 1])
        m.then_inc(J.read[who], 1)


def dve_diag(k, v, col, n):
    v.tensor_tensor(k.diag[:, :, :], bc(k.c["ident"].unsqueeze(1), KT, P), bc(col.unsqueeze(2), KT, P), ALU.mult)\
     .then_inc(k.diag_ready.sem, 1)


def dve_post_norm(k, v, sd, J, n, it=None):
    J.evac(v, ("g", 1), it)
    for tb in range(TB):
        for half in range(2):
            t = k.ptmp[half]
            xs = k.x[:, tb, half * 512:(half + 1) * 512]
            sd.link(v.tensor_tensor(t, k.psum[4 + 2 * tb + half][:, :], k.gbc[:, half * 512:(half + 1) * 512], ALU.mult))
            sd.link(v.scalar_tensor_tensor(xs, xs, ALPHA, t, ALU.mult, ALU.add))
            sd.done(v.bn_stats(k.bn[:, tb, half, :], xs))
        sd.settle()
        m = v.bn_aggr(k.mv[:, tb, :], k.bn[:, tb, :, :])
        sd.done(m) if tb == 0 else m.then_inc(k.ln_var.sem, 1)
    v.wait_ge(k.ln_rstd.sem, n + 1)
    v.wait_ge(k.ln_loaded, 32 * (n + 1))
    for tb in range(TB):
        sd.done(v.tensor_scalar(k.x[:, tb, :], k.x[:, tb, :], k.mv[:, tb, 0:1], k.stat[:, 12 + tb:13 + tb], ALU.subtract, ALU.mult))
    sd.settle()
    for tb in range(TB):
        sd.done(v.tensor_tensor(k.x[:, tb, :], k.x[:, tb, :], k.lng, ALU.mult))
    sd.settle()
    for tb in range(TB):
        m = v.tensor_tensor(k.x[:, tb, :], k.x[:, tb, :], k.lnb, ALU.add)
        sd.done(m) if tb == 0 else m.then_inc(k.x2_done.sem, 1)
    v.wait_ge(k.x2_done.sem, n + 1)
    sd.settle()


def dve_mla(k, v, sd):
    J, ps = k.J2, k.psum
    v.wait_ge(k.mla_loaded, 32)
    b = J.take(v, "dve", "mod")
    mods = shaped(ps[b][:, 0:192], 96, 2)
    sd.done(v.tensor_tensor(k.mod.rearrange("p a b -> p (a b)"), mods[:, :, 0], k.vec2[:, Y_BMOD:Y_BMOD + 96], ALU.add))
    v.tensor_tensor(k.cmod[:, :], mods[:, 0:16, 1], k.vec2[:, Y_BMOD:Y_BMOD + 16], ALU.add).then_inc(J.read["dve"], 1)
    J.evac(v, "mod")
    sd.settle()
    for l in range(2):
        sd.done(v.tensor_scalar(k.mod[:, l, SC1:SC1 + 8], k.mod[:, l, SC1:SC1 + 8], 1.0, None, ALU.add))
        sd.done(v.tensor_scalar(k.mod[:, l, SC2:SC2 + 8], k.mod[:, l, SC2:SC2 + 8], 1.0, None, ALU.add))
    v.tensor_scalar(k.cmod[:, 8:16], k.cmod[:, 8:16], 1.0, None, ALU.add).then_inc(k.mod_ready, 1)
    v.wait_ge(k.mod_ready, 1)
    sd.settle()
    mod_evac(k, v, J, "dve", "xt", lambda kt: k.hc[:, kt, 0:S], k.mod[:, 0, SH1:SH1 + 8], k.mod[:, 0, SC1:SC1 + 8])
    mod_evac(k, v, J, "dve", "ct", lambda kt: k.hc[:, kt, S:TOK], k.cmod[:, 0:8], k.cmod[:, 8:16])
    dve_diag(k, v, k.mod[:, 0, G1:G1 + 8], 1)
    J.evac(v, "sq")
    sd.link(v.reciprocal(k.rq, k.rq))
    for i in range(3):
        m = v.scalar_tensor_tensor(k.zq[:, i, :], k.zq[:, i, :], k.vec2[:, Y_QN + i:Y_QN + i + 1], k.rq, ALU.mult, ALU.mult)
        sd.done(m) if i < 2 else m.then_inc(k.cq_ready, 1)
    J.evac(v, "sk")
    sd.link(v.reciprocal(k.rkv, k.rkv))
    for i in range(2):
        m = v.scalar_tensor_tensor(k.zkv[:, i, :], k.zkv[:, i, :], k.vec2[:, Y_KVN + i:Y_KVN + i + 1], k.rkv, ALU.mult, ALU.mult)
        sd.done(m) if i < 1 else m.then_inc(k.ckv_ready, 1)
    b = J.take(v, "dve", "rk")
    v.tensor_tensor(k.krot, ps[b][:, 0:S], k.sin, ALU.mult).then_inc(J.read["dve"], 1)
    J.evac(v, "rk")
    sd.link(v.tensor_tensor(k.kr[:, 0:S], k.kr[:, 0:S], k.cos, ALU.mult))
    v.tensor_tensor(k.kr[:, 0:S], k.kr[:, 0:S], k.krot, ALU.add).then_inc(k.rope_ready, 1)
    for i in range(2):
        b = J.take(v, "dve", ("rq", i))
        v.tensor_tensor(k.qrot[:, 2 * i:2 * i + 2, :], shaped(ps[b][:, :], 2, S), bc(k.sin.unsqueeze(1), 2, S), ALU.mult)\
         .then_inc(J.read["dve"], 1)
    J.evac(v, ("rq", 1))
    sd.link(v.tensor_tensor(k.qr[:, :, :], k.qr[:, :, :], bc(k.cos.unsqueeze(1), 4, S), ALU.mult))
    v.tensor_tensor(k.qr[:, :, :], k.qr[:, :, :], k.qrot[:, :, :], ALU.add).then_inc(k.rope_ready, 1)
    for h in range(1, MH, 2):
        b = J.take(v, "dve", ("uk", h))
        v.tensor_copy(k.kn[:, h, :], ps[b][:, :]).then_inc(J.read["dve"], 1)
    for i in range(1, 8, 2):
        b = J.take(v, "dve", ("uv", i))
        v.tensor_copy(k.vv[:, i // 2, 512:1024], ps[b][:, :]).then_inc(J.read["dve"], 1)

    def maximum(n):
        b = J.peek(v, ("s", n))
        sd.link(v.tensor_reduce(k.amx[:, n:n + 1], ps[b][:, :], AX.X, ALU.max))
        v.tensor_scalar(k.amx[:, n:n + 1], k.amx[:, n:n + 1], -SCALE, None, ALU.mult).then_inc(k.s_max, 1)

    maximum(0)
    for n in range(2 * MH):
        if n + 1 < 2 * MH:
            maximum(n + 1)
        J.evac(v, ("s", n))
        sd.link(v.reciprocal(k.asum[:, n:n + 1], k.asum[:, n:n + 1]))
        v.tensor_scalar(k.p[n % 2], k.p[n % 2], k.asum[:, n:n + 1], None, ALU.mult).then_inc(k.p_ready, 1)
        if n % 2:
            h = n // 2
            b = J.take(v, "dve", ("o", h))
            v.tensor_copy(k.oT[:, h, :], ps[b][:, 0:S]).then_inc(J.read["dve"], 1)
    v.wait_ge(k.y2_acc.sem, 1)
    dve_post_norm(k, v, sd, J, 0)


def dve_top16(k, v, sd, src, spare, val, idx, n):
    for h in range(n):
        sd.done(v.max(val[:, h, 0:8], src(h)))
    sd.settle()
    for h in range(n):
        sd.done(v.match_replace(spare(h), val[:, h, 0:8], src(h), NEG))
        sd.done(v.max_index(idx[:, h, 0:8], val[:, h, 0:8], src(h)))
    sd.settle()
    for h in range(n):
        sd.done(v.max(val[:, h, 8:16], spare(h)))
    sd.settle()
    for h in range(n):
        sd.done(v.max_index(idx[:, h, 8:16], val[:, h, 8:16], spare(h)))
    sd.settle()


def dve_peer(k, v, sd, l):
    J = k.J3
    mod_evac(k, v, J, "dve", "xt", lambda kt: k.hT[:, kt, :], k.mod[:, l, SH2:SH2 + 8], k.mod[:, l, SC2:SC2 + 8], l)
    for i in range(1, 8, 2):
        b = J.take(v, "dve", ("q", i), l)
        v.tensor_copy(k.qT[:, 2 * i:2 * i + 2, :], shaped(k.psum[b][:, :], 2, S)).then_inc(J.read["dve"], 1)
    for tb in range(TB):
        J.evac(v, ("s", 4 * tb + 3), l)
        dve_top16(k, v, sd, lambda h: k.s[:, tb, h, :], lambda h: k.s2[:, h, :], k.val, k.ix, HH)
        sd.done(v.tensor_copy(k.ixf[:, :, :], k.ix[:, :, :]))
        val = k.val.rearrange("p (h a) k -> p h a k", a=2)
        ixf = k.ixf.rearrange("p (h a) k -> p h a k", a=2)
        cand = k.cand.rearrange("p h (a b) -> p h a b", b=TOPK)
        sd.link(v.tensor_tensor(cand, bc(val[:, :, 0, :].unsqueeze(3), PH, TOPK, TOPK), bc(val[:, :, 1, :].unsqueeze(2), PH, TOPK, TOPK),
                                ALU.add))
        dve_top16(k, v, sd, lambda h: k.cand[:, h, :], lambda h: k.cand2[:, h, :], k.top, k.pos, PH)
        v.tensor_tensor(k.sel[:, tb, 2, :, :], k.top[:, :, :], bc(k.top[:, :, 0:1], PH, TOPK), ALU.subtract).then_inc(k.gate2_arg.sem, 1)
        sd.done(v.tensor_scalar(k.pa_[:, :, :], k.pos[:, :, :], 4, None, ALU.logical_shift_right))
        sd.link(v.tensor_scalar(k.pb_[:, :, :], k.pos[:, :, :], 15, None, ALU.bitwise_and))
        sd.done(v.tensor_copy(k.posa[:, :, :], k.pa_[:, :, :]))
        sd.link(v.tensor_copy(k.posb[:, :, :], k.pb_[:, :, :]))
        eq = k.eq.rearrange("p h (a b) -> p h a b", b=TOPK)
        for a, pos in enumerate((k.posa, k.posb)):
            sd.link(v.tensor_tensor(eq, bc(k.c["iota"][:, 0:TOPK].unsqueeze(1).unsqueeze(1), PH, TOPK, TOPK),
                                    bc(pos[:, :, :].unsqueeze(3), PH, TOPK, TOPK), ALU.is_equal))
            sd.link(v.tensor_tensor(eq, eq, bc(ixf[:, :, a, :].unsqueeze(2), PH, TOPK, TOPK), ALU.mult))
            sd.link(v.tensor_reduce(k.sel[:, tb, a, :, :], eq, AX.X, ALU.add))
        v.wait_ge(k.gate2_exp.sem, k.gate2_exp.at(tb + 1, l))
        sd.link(v.tensor_reduce(k.gsum[:, :], k.sel[:, tb, 2, :, :], AX.X, ALU.add))
        sd.link(v.reciprocal(k.gsum[:, :], k.gsum[:, :]))
        v.tensor_tensor(k.sel[:, tb, 2, :, :], k.sel[:, tb, 2, :, :], bc(k.gsum[:, :].unsqueeze(2), PH, TOPK), ALU.mult)\
         .then_inc(k.sel_ready.sem, 1)
    J.evac(v, ("rt", 1), l)
    base = l * W_GROUPS

    def onehots(i, u, first):
        if not first:
            v.wait_ge(k.w_filled, i * 4 + (base + u - 1))
        hot = k.hot[u % 2]
        v.tensor_tensor(hot[:, 0, :, :], bc(k.c["iota"].unsqueeze(1), 4, P),
                        bc(k.rT[:, 1, bass.ds(i * 16 + u * 4, 4)].unsqueeze(2), 4, P), ALU.is_equal)
        for t in range(4):
            col = i * 16 + (u * 4 + t)
            m = v.tensor_scalar(hot[:, 1, t, :], k.c["iota"], k.rT[:, 0, bass.ds(col, 1)], k.rT[:, 2, bass.ds(col, 1)],
                                ALU.is_equal, ALU.mult)
        m.then_inc(k.hot_ready, 1)

    for u in range(4):
        onehots(0, u, u < 2)
    with v.Fori(1, W_GROUPS // 4) as i:
        for u in range(4):
            onehots(i, u, False)
    v.wait_ge(k.w_read, base + W_GROUPS)
    dve_experts(k, v, f"exp{l}", EXP_SLOTS, k.PX, l,
                lambda i, u: k.W[:, :, bass.ds(i * 4 + u, 1)].rearrange("p t a -> p (t a)"), static=True)
    v.wait_ge(k.y_exp.sem, l + 1)
    dve_diag(k, v, k.mod[:, l, G2:G2 + 8], 2 * l + 2)
    dve_post_norm(k, v, sd, J, 2 * l + 1, l)


def dve_pool(k, v, sd):
    J = k.J4
    L = k.LZ
    v.memset(k.zp[:, :, :], 0.0).then_inc(k.zp_cleared, 1)
    mod_evac(k, v, J, "dve", "xt", lambda kt: k.hT[:, kt, :], k.mod[:, 1, SH1:SH1 + 8], k.mod[:, 1, SC1:SC1 + 8])
    dve_diag(k, v, k.mod[:, 1, G1:G1 + 8], 3)
    for g, w in enumerate(WINDOWS):
        J.evac(v, ("z", g))
        src, n, step, flip = k.zp[:, 2 * g:2 * g + 2, :], L, 1, 0
        while step < w:
            n -= step
            dst = k.za[flip]
            sd.link(v.tensor_tensor(dst[:, :, 0:n], src[:, :, 0:n], src[:, :, step:step + n], ALU.add))
            src, step, flip = dst, step * 2, 1 - flip
        first = 8 - w // 2
        if g == 0:
            v.wait_ge(k.counts_loaded, 16)
        sd.link(v.tensor_tensor(k.pooled[:, 2 * g:2 * g + 2, :], src[:, :, first:first + S], bc(k.inv_count[:, g:g + 1, :], 2, S), ALU.mult))
        v.tensor_tensor(k.pooled[:, 2 * g:2 * g + 2, :], k.pooled[:, 2 * g:2 * g + 2, :], k.zp[:, 2 * g:2 * g + 2, 8:8 + S],
                        ALU.subtract).then_inc(k.pooled_ready, 1)
    for g in (1, 3):
        b = J.take(v, "dve", ("gp", g))
        for dt in range(2):
            m = v.tensor_scalar(k.hT[:, 2 * g + dt, :], k.psum[b][:, dt * S:(dt + 1) * S],
                                k.vec2[:, Y_PS + 2 * g + dt:Y_PS + 2 * g + dt + 1], None, ALU.mult)
        m.then_inc(J.read["dve"], 1)
    v.wait_ge(k.y2_acc.sem, 2)
    dve_post_norm(k, v, sd, J, 2)


def act_gate_row(k, a, J, n, it=None):
    for i in range(2):
        a.dma_start((k.lng, k.lnb)[i], k.dram["ln"][n:n + 1, i * D:(i + 1) * D].to_broadcast([P, D])).then_inc(k.ln_loaded, 16)
    for i in range(2):
        b = J.take(a, "act", ("g", i), it)
        a.activation(k.gbc[:, i * 512:(i + 1) * 512], k.psum[b][:, :], ACT.Copy).then_inc(J.read["act"], 1)


def act_mla(k, a, sa):
    J, ps = k.J2, k.psum
    a.dma_start(k.vec2[:, :], k.dram["vec2"]).then_inc(k.mla_loaded, 16)
    a.dma_start(k.ctx[:, :, :], k.dram["ctx"].rearrange("(t p) d -> p t d", p=P)).then_inc(k.mla_loaded, 16)
    a.wait_ge(k.mla_loaded, 32)
    a.activation(k.cs[:, :, :], shaped(k.vec2[:, Y_C:Y_C + 16], KT, 2), ACT.Silu).then_inc(k.c_ready, 1)
    with a.Fori(0, MOD_SLOTS // 4) as i:
        for u in range(2):
            a.wait_ge(k.weights_used, i * 4 + STREAM.used("mod", 2 * u + 1))
            a.activation(k.mod_row[:, bass.ds(i * 1024 + u * 512, 512)], ps[4 + u][0:2, :], ACT.Copy).then_inc(k.mod_read, 1)
    a.wait_ge(k.mod_ready, 1)
    mod_evac(k, a, J, "act", "xt", lambda kt: k.hc[:, kt, 0:S], k.mod[:, 0, SH1:SH1 + 8], k.mod[:, 0, SC1:SC1 + 8])
    mod_evac(k, a, J, "act", "ct", lambda kt: k.hc[:, kt, S:TOK], k.cmod[:, 0:8], k.cmod[:, 8:16])

    def copy(key, dst, n, **kw):
        b = J.take(a, "act", key)
        a.activation(dst, n(ps[b]) if callable(n) else ps[b][:, 0:n], kw.pop("func", ACT.Copy), **kw).then_inc(J.read["act"], 1)

    for i in range(3):
        copy(("zq", i), k.zq[:, i, :], S)
    J.evac(a, ("zq", 2))
    a.activation(k.zsq[:, :, :], k.zq[:, :, :], ACT.Square).then_inc(k.z_squares, 1)
    for i in range(2):
        copy(("zk", i), k.zkv[:, i, :], TOK)
    copy("zr", k.kr, TOK)
    J.evac(a, "zr")
    a.activation(k.zksq[:, :, :], k.zkv[:, :, :], ACT.Square).then_inc(k.z_squares, 1)
    copy("sq", k.rq, S, func=ACT.Sqrt, scale=1.0 / QR, bias=k.eps6)
    copy("sk", k.rkv, TOK, func=ACT.Sqrt, scale=1.0 / KVR, bias=k.eps6)
    for i in range(6):
        dst = k.qn[:, 2 * i:2 * i + 2, :] if i < 4 else k.qr[:, 2 * i - 8:2 * i - 6, :]
        copy(("uq", i), dst, lambda t: shaped(t[:, :], 2, S))
    for h in range(0, MH, 2):
        copy(("uk", h), k.kn[:, h, :], TOK)
    for i in range(0, 8, 2):
        copy(("uv", i), k.vv[:, i // 2, 0:512], 512)
    def soft(n):
        a.wait_ge(k.s_max, n + 1)
        if n >= 2:
            J.evac(a, ("pt", n - 2))
        b = J.take(a, "act", ("s", n))
        a.activation(k.p[n % 2], ps[b][:, :], ACT.Exp, bias=k.amx[:, n:n + 1], scale=SCALE,
                     accum_out=k.asum[:, n:n + 1]).then_inc(J.read["act"], 1)

    soft(0)
    soft(1)
    for n in range(2 * MH):
        h, qb = n // 2, n % 2
        copy(("pt", n), k.pT[h % 2][:, :, qb * P:(qb + 1) * P], lambda t: shaped(t[:, :], 4, P))
        if n + 2 < 2 * MH:
            soft(n + 2)
    act_gate_row(k, a, J, 0)


def act_peer(k, a, sa, l):
    J = k.J3
    a.wait_ge(k.x2_done.sem, 2 * l + 1)
    mod_evac(k, a, J, "act", "xt", lambda kt: k.hT[:, kt, :], k.mod[:, l, SH2:SH2 + 8], k.mod[:, l, SC2:SC2 + 8], l)
    for i in range(0, 8, 2):
        b = J.take(a, "act", ("q", i), l)
        a.activation(k.qT[:, 2 * i:2 * i + 2, :], shaped(k.psum[b][:, :], 2, S), ACT.Copy).then_inc(J.read["act"], 1)
    for i in range(8):
        tb, part = i // 4, i % 4
        b = J.take(a, "act", ("s", i), l)
        a.activation(k.s[:, tb, 4 * part:4 * part + 4, :], shaped(k.psum[b][:, :], 4, NK), ACT.Copy).then_inc(J.read["act"], 1)
    for tb in range(TB):
        a.wait_ge(k.gate2_arg.sem, k.gate2_arg.at(tb + 1, l))
        a.activation(k.sel[:, tb, 2, :, :], k.sel[:, tb, 2, :, :], ACT.Exp).then_inc(k.gate2_exp.sem, 1)
    for i, (arr, n) in enumerate(((0, 2), (2, 1))):
        b = J.take(a, "act", ("rt", i), l)
        a.activation(k.rT[:, arr:arr + n, :], shaped(k.psum[b][:, 0:n * S], n, S), ACT.Copy).then_inc(J.read["act"], 1)
    base = l * W_GROUPS
    with a.Fori(0, W_GROUPS // 4) as i:
        for u in range(4):
            a.wait_ge(k.w_filled, i * 4 + (base + u + 1))
            a.activation(k.W[:, bass.ds(i * 16 + u * 4, 4), :], shaped(k.psum[u][:, :], 4, P), ACT.Copy).then_inc(k.w_read, 1)
    act_experts(k, a, EXP_SLOTS, k.PX, l, ACT.Gelu)
    a.wait_ge(k.y_exp.sem, l + 1)
    act_gate_row(k, a, J, 2 * l + 1, l)


def act_pool(k, a, sa):
    J = k.J4
    a.wait_ge(k.x2_done.sem, 2)
    a.dma_start(k.inv_count[:, :, :], k.dram["const"][:, C_POOL:CONST].rearrange("p (w s) -> p w s", s=S)).then_inc(k.counts_loaded, 16)
    mod_evac(k, a, J, "act", "xt", lambda kt: k.hT[:, kt, :], k.mod[:, 1, SH1:SH1 + 8], k.mod[:, 1, SC1:SC1 + 8])
    a.wait_ge(k.zp_cleared, 1)
    for i in range(4):
        b = J.take(a, "act", ("z", i))
        a.activation(k.zp[:, 2 * i:2 * i + 2, 8:8 + S], shaped(k.psum[b][:, :], 2, S), ACT.Copy).then_inc(J.read["act"], 1)
    for g in (0, 2):
        b = J.take(a, "act", ("gp", g))
        for dt in range(2):
            m = a.activation(k.hT[:, 2 * g + dt, :], k.psum[b][:, dt * S:(dt + 1) * S], ACT.Copy,
                             scale=k.vec2[:, Y_PS + 2 * g + dt:Y_PS + 2 * g + dt + 1])
        m.then_inc(J.read["act"], 1)
    act_gate_row(k, a, J, 2)


def pool_ln_rstd(k, p, sp, n):
    p.wait_ge(k.ln_var.sem, n + 1)
    sp.link(p.tensor_scalar(k.stat[:, 12:14], k.mv[:, :, 1], 1.0, LN_EPS, ALU.mult, ALU.add))
    p.tensor_tensor(k.stat[:, 12:14], k.stat[:, 12:14], k.minus_half.to_broadcast([P, 2]), ALU.pow).then_inc(k.ln_rstd.sem, 1)
    p.wait_ge(k.ln_rstd.sem, n + 1)


LN_EPS = 1e-5


def sp_second(k, sp):
    def load(r, src):
        sp.dma_start(k.ring[r], src).then_inc(k.weights_loaded[r], 16)

    def used(g):
        sp.wait_ge(k.weights_used, g + 1)

    with sp.Fori(1, MOD_SLOTS // 4) as i:
        for u in range(4):
            sp.wait_ge(k.weights_used, i * 4 + (STREAM.used("mod", u) - 4))
            load(u, k.dram["w1"][bass.ds(i * 4 + (DEPTH * LAYER_SLOTS + u), 1)].rearrange("a p n -> (a p) n"))
    for seg, n, off in (("mla", MLA_SLOTS, 0), ("qk0", QK_SLOTS, 12), ("exp0", EXP_SLOTS, 0), ("pool", POOL_SLOTS, 21),
                        ("qk1", QK_SLOTS, 30), ("exp1", EXP_SLOTS, 1)):
        src = k.dram["w2"][off:off + n] if n != EXP_SLOTS else k.dram["experts"][off]
        for pos in range(min(n, RING)):
            used(STREAM.prior[(seg, 0, pos)])
            load(pos, src[pos])
        if n == EXP_SLOTS:
            with sp.Fori(1, n // 4) as i:
                for u in range(4):
                    sp.wait_ge(k.weights_used, i * 4 + (STREAM.used(seg, u) - 4))
                    load(u, src[bass.ds(i * 4 + u, 1)].rearrange("a p n -> (a p) n"))
        else:
            for pos in range(RING, n):
                used(STREAM.base[seg] + pos - RING)
                load(pos % RING, src[pos])


class Pass:

    def __init__(self, k, ctx, nc, name, n, at, hi):
        names = ("up", "acted", "weighted", "u_split", "v_split", "h_split", "chain")
        self.up, self.acted, self.weighted, self.u_split, self.v_split, self.h_split, self.chain = (
            ctx.enter_context(nc.semaphore(f"{name}_{s}")) for s in names)
        self.n = n
        self.r, self.g = ([k.sb[:, at + (2 * j + i) * S:at + (2 * j + i + 1) * S] for i in range(2)] for j in range(2))
        hidden = k.alias(f"{name}_hidden", at, 4 * S)
        self.gh, self.gl = ([hidden[:, (2 * j + i) * S:(2 * j + i + 1) * S] for i in range(2)] for j in range(2))
        high = k.alias(f"{name}_high", hi, SPLIT)
        self.hh = shaped(high[:, 0:KT * S], KT, S)
        self.uh, self.vh = ([high[:, KT * S + (2 * j + i) * D:KT * S + (2 * j + i + 1) * D] for i in range(2)] for j in range(2))

    def base(self, lay):
        return lay * self.n


def build(nc, dram, out):
    with ExitStack() as ctx:
        k = Ctx()
        k.dram = dram
        plan_memory(nc, ctx, k)
        plan_memory2(k)
        sem = lambda n: ctx.enter_context(nc.semaphore(n))
        sig = lambda n, per: Sig(ctx, nc, n, per)
        k.h_squares = sig("h_squares", 4)
        k.h_rstd = sig("h_rstd", 2)
        k.h_scaled = sig("h_scaled", 4)
        k.state_zeroed = sig("state_zeroed", 1)
        k.lam_arg = sig("lam_arg", 1)
        k.lam_exp = sig("lam_exp", 1)
        k.sub_ready = sig("sub_ready", 1)
        k.gate_arg = sig("gate_arg", 1)
        k.gate_exp = sig("gate_exp", 1)
        k.g_ready = sig("g_ready", 1)
        k.sconv = sig("sconv", 1)
        k.gc_ready = sig("gc_ready", 1)
        k.gc_exp = sig("gc_exp", 1)
        k.beg_ready = sig("beg_ready", 1)
        k.sq_ready = sig("sq_ready", 1)
        k.qk_normed = sig("qk_normed", 1)
        k.sc_max = sig("sc_max", NMAP)
        k.sc_exp = sig("sc_exp", NMAP)
        k.sc_exp2 = sig("sc_exp2", NMAP)
        k.attn_ready = sig("attn_ready", DH)
        k.od_sq = sig("od_sq", 1)
        k.od_ss = sig("od_ss", 1)
        k.od_rstd = sig("od_rstd", 1)
        k.od_ready = sig("od_ready", 1)
        k.E_exp = sig("E_exp", GRP)
        k.ES_ready = sig("ES_ready", GRP)
        k.D_ready = sig("D_ready", 1)
        k.P0_ready = sig("P0_ready", 1)
        k.LT_ready = sig("LT_ready", 3 * GRP)
        k.kv_scaled = sig("kv_scaled", 1)
        k.conv_done = sig("conv_done", 1)
        k.csq_ready = sig("csq_ready", 1)
        k.conv_lin = sig("conv_lin", 1)
        k.conv_out = sig("conv_out", 1)
        k.o_sq = sig("o_sq", 1)
        k.o_ss = sig("o_ss", 1)
        k.o_rstd = sig("o_rstd", 1)
        k.o_ready = sig("o_ready", 1)
        k.y_acc = sig("y_acc", 1)
        k.y_ff = sig("y_ff", 1)
        k.y_squares = sig("y_squares", 8)
        k.y_rstd = sig("y_rstd", 2)
        k.x_mixed = sig("x_mixed", 1)
        k.x_done = sig("x_done", 1)
        k.diag_ready = sig("diag_ready", 4)
        k.y2_acc = sig("y2_acc", 2)
        k.x2_done = sig("x2_done", 4)
        k.ln_var = sig("ln_var", 4)
        k.ln_rstd = sig("ln_rstd", 4)
        k.y_exp = sig("y_exp", 2)
        k.sel_ready = sig("sel_ready", 2)
        k.gate2_arg = sig("gate2_arg", 2)
        k.gate2_exp = sig("gate2_exp", 2)
        k.c_ready = sem("c_ready")
        k.mod_ready = sem("mod_ready")
        k.mla_loaded = sem("mla_loaded")
        k.z_squares = sem("z_squares")
        k.cq_ready = sem("cq_ready")
        k.ckv_ready = sem("ckv_ready")
        k.rope_ready = sem("rope_ready")
        k.s_max = sem("s_max")
        k.p_ready = sem("p_ready")
        k.hot_ready = sem("hot_ready")
        k.w_filled = sem("w_filled")
        k.w_read = sem("w_read")
        k.pooled_ready = sem("pooled_ready")
        k.ln_loaded = sem("ln_loaded")
        k.zp_cleared = sem("zp_cleared")
        k.dve2_step = sem("dve2_step")
        k.pool2_step = sem("pool2_step")
        k.dve_step = sem("dve_step")
        k.act_step = sem("act_step")
        k.pool_step = sem("pool_step")
        k.weights_used = sem("weights_used")
        k.params_loaded = sem("params_loaded")
        k.post_loaded = sem("post_loaded")
        k.start_loaded = sem("start_loaded")
        k.zeroed = sem("zeroed")
        k.stored = sem("stored")
        k.counts_loaded = sem("counts_loaded")
        k.mod_read = sem("mod_read")
        k.weights_loaded = [sem(f"weights_loaded{r}") for r in range(RING)]
        k.J1 = Jobs(layer_jobs()).sems(ctx, nc, "layer")
        k.J2 = Jobs(mla_jobs()).sems(ctx, nc, "mla")
        k.J3 = Jobs(peer_jobs()).sems(ctx, nc, "peer")
        k.J4 = Jobs(pool_jobs()).sems(ctx, nc, "pool")
        k.PX = Pass(k, ctx, nc, "peer_pass", EXP_SLOTS, k.exp_at, k.late)
        k.FF = Pass(k, ctx, nc, "ff", FF_SLOTS, k.ff_at, k.ff_hi)
        block = ctx.enter_context(nc.Block())

        @block.sync
        def _(sp):
            sp.dma_start(k.x[:, :, :], dram["x"].rearrange("(t p) d -> p t d", p=P)).then_inc(k.start_loaded, 16)
            sp.dma_start(k.const[:, :], dram["const"][:, 0:C_POOL]).then_inc(k.start_loaded, 16)
            sp_layers(k, sp)
            sp_second(k, sp)
            sp.wait_ge(k.x2_done.sem, 2 * DEPTH)
            sp.dma_start(out.rearrange("(t p) d -> p t d", p=P), k.x[:, :, :]).then_inc(k.stored, 16)
            sp.wait_ge(k.stored, 16)

        @block.tensor
        def _(pe):
            pe.wait_ge(k.start_loaded, 32)
            pe.wait_ge(k.zeroed, 2)
            with pe.Fori(0, DEPTH) as lay:
                pe_layer(k, pe, lay)
            pe_mla(k, pe)
            pe_peer(k, pe, 0)
            pe_pool(k, pe)
            pe_peer(k, pe, 1)

        @block.vector
        def _(v):
            v.memset(k.zero[:, :], 0.0).then_inc(k.zeroed, 1)
            v.memset(k.zero_row[:, :], 0.0).then_inc(k.zeroed, 1)
            v.wait_ge(k.start_loaded, 32)
            with v.Fori(0, DEPTH) as lay:
                dve_layer(k, v, lay)
            sd = Steps(v, k.dve2_step, 0)
            dve_mla(k, v, sd)
            dve_peer(k, v, sd, 0)
            dve_pool(k, v, sd)
            dve_peer(k, v, sd, 1)

        @block.scalar
        def _(a):
            a.wait_ge(k.start_loaded, 32)
            with a.Fori(0, DEPTH) as lay:
                act_layer(k, a, lay)
            act_mla(k, a, None)
            act_peer(k, a, None, 0)
            act_pool(k, a, None)
            act_peer(k, a, None, 1)

        @block.gpsimd
        def _(p):
            p.wait_ge(k.start_loaded, 32)
            with p.Fori(0, DEPTH) as lay:
                pool_layer(k, p, lay)
            st2 = Steps(p, k.pool2_step, 0)
            for n in range(2 * DEPTH):
                pool_ln_rstd(k, p, st2, n)


def tiles_t(w):
    kk, m = w.shape
    return w.reshape(kk // P, P, m // P, P).transpose(2, 1, 0, 3).reshape(m // P, P, kk)


def in_slots(parts):
    out, row, used = [], [], 0
    for a in parts:
        if used + a.shape[1] > SLOT:
            out.append(row)
            row, used = [], 0
        row.append(a)
        used += a.shape[1]
    out.append(row)
    full = np.zeros((len(out), P, SLOT), np.float32)
    for i, r in enumerate(out):
        c = 0
        for a in r:
            full[i, :, c:c + a.shape[1]] = a
            c += a.shape[1]
    return full


def natural(w):
    kk, n = w.shape
    t = w.reshape(kk // P, P, n)
    return [np.concatenate([t[2 * s], t[2 * s + 1]], 1) for s in range(kk // P // 2)]


def layer_slots(i, l):
    w = i["w_in"][l]
    o = np.cumsum([0, 512, 384, 384, 384, 1152, 384, 24])
    conv, dq, dk, dv, gq, gz, ba = (w[:, o[j]:o[j + 1]] for j in range(7))
    nat = in_slots(natural(np.concatenate([gz, ba, dv], 1)))
    t = tiles_t(np.concatenate([gq, conv, dq, dk], 1))
    pairs = [(0, 1), (2, 3), (4, 5), (6, 7), (8,), (11, 12), (9, 10), (13, 14), (15, 16), (17, 18)]
    tr = [np.concatenate([t[j] for j in p] + ([np.zeros_like(t[0])] if len(p) == 1 else []), 1) for p in pairs]
    wo = in_slots(natural(i["w_out"][l]))
    ff = np.concatenate([tiles_t(i["w_ff1"][l]), i["w_ff2"][l].reshape(FF_SLOTS, P, D)], 2)
    return [nat, np.stack(tr), wo, ff]


def cols(v):
    return v.reshape(-1, P).T


def lay_out(i):
    f = lambda a: np.asarray(a)
    i = {n: f(a) for n, a in i.items()}
    w1 = []
    vec, row, post = [], [], []
    for l in range(DEPTH):
        w1 += layer_slots(i, l)
        tap = i["conv_dw_w"][l].reshape(CONV_W, 2, P).transpose(2, 1, 0).reshape(P, 2 * CONV_W)
        dt = i["delta_conv_w"][l].reshape(3, 9, P).transpose(2, 1, 0).reshape(P, 27)
        two = lambda a: np.concatenate([a, a])[:, None]
        vec.append(np.concatenate([cols(i["pre_mix_w"][l]), cols(i["pre_mlp_w"][l]), tap, cols(i["conv_dw_b"][l]),
                                   cols(i["conv_ln_w"][l]), cols(i["conv_ln_b"][l]), two(i["diff_subln_w"][l]),
                                   two(i["delta_norm_w"][l]), dt], 1))
        init = np.array([0.8 - 0.6 * math.exp(-0.3 * l)], np.float32)
        row.append(np.concatenate([i["diff_lambda_q1"][l], i["diff_lambda_k1"][l], i["diff_lambda_q2"][l], i["diff_lambda_k2"][l],
                                   i["delta_A_log"][l].reshape(-1), i["delta_dt_bias"][l].reshape(-1), init]))
        post.append(np.concatenate([i["post_mix_w"][l], i["post_mlp_w"][l]]))
    for l in range(DEPTH):
        w1.append(i["w_mod_2"][l].reshape(2, 4, P, 12, 512).transpose(3, 0, 2, 1, 4).reshape(24, P, SLOT))
    w = i["mla_w_uq_2"][0].reshape(QR, MH, NOPE + ROPE)
    uq = np.concatenate([w[:, :, :NOPE].reshape(QR, -1), w[:, :, NOPE:].reshape(QR, -1)], 1)
    w = i["mla_w_ukv_2"][0].reshape(KVR, MH, NOPE + VD)
    uk, uv = w[:, :, :NOPE].reshape(KVR, -1), w[:, :, NOPE:].reshape(KVR, -1)
    win = i["mla_w_in_2"][0]
    win = np.concatenate([win, win[:, QR + KVR:]], 1)
    w2 = [in_slots(tiles_t(win)), in_slots(tiles_t(uq)), in_slots([np.concatenate(list(tiles_t(uk)), 1)]),
          in_slots(natural(uv)), in_slots(natural(i["mla_w_o_2"][0]))]
    keys = np.stack([i["peer_k1_2"], i["peer_k2_2"]], 2)
    qk = [[in_slots(tiles_t(i["peer_w_q_2"][l])), keys[l].transpose(3, 0, 1, 2).reshape(1, P, SLOT)] for l in range(DEPTH)]
    grp = i["pool_w_grp_2"][0].reshape(4, 2, P, 2, P).transpose(2, 0, 3, 1, 4).reshape(1, P, SLOT)
    w2 += qk[0] + [in_slots(tiles_t(i["pool_w_in_2"][0])), grp, in_slots(natural(i["pool_w_out_2"][0]))] + qk[1]
    experts = np.empty((DEPTH, EXP_SLOTS, P, 2, D), np.float32)
    for l in range(DEPTH):
        experts[l, :, :, 0] = i["peer_u_2"][l].reshape(EXP_SLOTS, P, KT, P).transpose(0, 3, 2, 1).reshape(EXP_SLOTS, P, D)
        experts[l, :, :, 1] = i["peer_v_2"][l].reshape(EXP_SLOTS, P, D)
    c2 = np.stack([cols(i["c_2"][0]), cols(i["c_ctx_2"])], 2).reshape(P, 16)
    vec2 = np.concatenate([c2] + [cols(i["b_mod_2"][l]) for l in range(DEPTH)] + [cols(i["mla_q_norm_2"][0]), cols(i["mla_kv_norm_2"][0]),
                          cols(i["pool_scale_2"][0])], 1)
    ln = np.stack([i["ln_g_2"], i["ln_b_2"]], 2).reshape(2 * DEPTH, 2 * D)
    return {
        "w2": np.concatenate(w2), "experts": experts.reshape(DEPTH, EXP_SLOTS, P, SLOT), "vec2": vec2, "ln": ln, "ctx": i["ctx_2"][0],
        "x": i["x"][0], "const": constants(), "w1": np.concatenate(w1), "vec1": np.stack(vec), "row1": np.stack(row),
        "post1": np.stack(post),
    }


def kernel(**inputs):
    import concourse.bacc as bacc
    from concourse.bass_utils import run_bass_kernel_spmd

    nc = bacc.Bacc("TRN2", target_bir_lowering=False, num_devices=1)
    arrays = {n: np.ascontiguousarray(a) for n, a in lay_out(inputs).items()}
    dram = {n: nc.dram_tensor(f"in_{n}", a.shape, mybir.dt.from_np(a.dtype), kind="ExternalInput").ap() for n, a in arrays.items()}
    out = nc.dram_tensor("out_x", (S, D), F32, kind="ExternalOutput").ap()
    build(nc, dram, out)
    r = run_bass_kernel_spmd(nc, [{f"in_{n}": a for n, a in arrays.items()}], core_ids=[0])
    return r.results[0]["out_x"].reshape(1, S, D)
```
